# Optimizing a Trainium2 kernel written in Bass

```python
import math
import jax
import jax.numpy as jnp
from jax import lax
import numpy as np

D_MODEL = 2048
BATCH = 1
SEQ = 512
DEPTH = 1
DEC_BATCH = 8
DEC_SEQ = 8
PAST_LEN = 1024
PAGE_SIZE = 128

HEAD_DIM = 128
ATTN_WIDTH = D_MODEL // 2
N_HEADS = ATTN_WIDTH // HEAD_DIM
LRU_WIDTH = D_MODEL - ATTN_WIDTH
LRU_BLOCKS = 8
LRU_BLOCK_W = LRU_WIDTH // LRU_BLOCKS
LRU_CONV_W = 4
LRU_C = 8.0
D_FF = 3 * D_MODEL
FFN_CONV_W = 3
Q_BLOCK = 128
N_MOD = 6
EPS = 1e-6
SB_SCALE = 1.0 / math.sqrt(HEAD_DIM)
SB_BIAS_INIT = -5.0
N_IN = 3 * ATTN_WIDTH + 2 * LRU_WIDTH

kernel_name = 'hymba_stickbreak_rglru_convffn_step'

def _rmsnorm(x, g):
    xf = x.astype(jnp.float32)
    y = xf * lax.rsqrt(jnp.mean(xf * xf, axis=-1, keepdims=True) + EPS)
    return y.astype(x.dtype) * g

def _causal_dwconv(x, prev, w, b):
    width = w.shape[0]
    t = x.shape[1]
    xp = jnp.concatenate([prev.astype(x.dtype), x], axis=1)
    y = b + w[0] * xp[:, 0:t]
    for i in range(1, width):
        y = y + w[i] * xp[:, i:i + t]
    return y, xp[:, -(width - 1):]

def _rglru(xc, h0, w_a, b_a, w_x, b_x, lam, reset_first):
    bsz, t, _ = xc.shape
    xf = xc.astype(jnp.float32)
    xb = xf.reshape(bsz, t, LRU_BLOCKS, LRU_BLOCK_W)
    r = jax.nn.sigmoid(jnp.einsum('btnc,ncd->btnd', xb, w_a.astype(jnp.float32)) + b_a).reshape(bsz, t, LRU_WIDTH)
    i = jax.nn.sigmoid(jnp.einsum('btnc,ncd->btnd', xb, w_x.astype(jnp.float32)) + b_x).reshape(bsz, t, LRU_WIDTH)
    log_a = -LRU_C * r * jax.nn.softplus(-lam.astype(jnp.float32))
    a = jnp.exp(log_a)
    mult = jnp.sqrt(-jnp.expm1(2.0 * log_a))
    if reset_first:
        mult = mult.at[:, 0].set(1.0)
    b = mult * i * xf
    b = b.at[:, 0].add(a[:, 0] * h0.astype(jnp.float32))

    def combine(left, right):
        a1, b1 = left
        a2, b2 = right
        return a1 * a2, a2 * b1 + b2

    _, h = lax.associative_scan(combine, (a, b), axis=1)
    return h, h[:, -1]

def _sb_prompt(q, k, v, bias):
    bsz, s, h, d = q.shape
    nb = s // Q_BLOCK
    qb = q.reshape(bsz, nb, Q_BLOCK, h, d).transpose(1, 0, 2, 3, 4)
    kpos = jnp.arange(s)
    vf = v.astype(jnp.float32)
    bh = bias.astype(jnp.float32)[None, :, None, None]

    def block(args):
        qi, idx = args
        z = jnp.einsum('bqhd,bkhd->bhqk', qi, k).astype(jnp.float32) * SB_SCALE + bh
        qpos = idx * Q_BLOCK + jnp.arange(Q_BLOCK)
        mask = kpos[None, :] < qpos[:, None]
        lm = jnp.where(mask, jax.nn.log_sigmoid(-z), 0.0)
        rc = lax.cumsum(lm, axis=3, reverse=True)
        w = jnp.where(mask, jnp.exp(jax.nn.log_sigmoid(z) + rc - lm), 0.0)
        return jnp.einsum('bhqk,bkhd->bqhd', w, vf)

    o = lax.map(block, (qb, jnp.arange(nb)))
    return o.transpose(1, 0, 2, 3, 4).reshape(bsz, s, h * d).astype(q.dtype)

def _sb_sample(q, k, v, bias, cache_k, cache_v, page_table):
    bsz, t, h, d = q.shape
    bh = bias.astype(jnp.float32)[None, :, None, None]
    z = jnp.einsum('bqhd,bkhd->bhqk', q, k).astype(jnp.float32) * SB_SCALE + bh
    tpos = jnp.arange(t)
    mask = tpos[None, :] < tpos[:, None]
    lm = jnp.where(mask, jax.nn.log_sigmoid(-z), 0.0)
    rc = lax.cumsum(lm, axis=3, reverse=True)
    w = jnp.where(mask, jnp.exp(jax.nn.log_sigmoid(z) + rc - lm), 0.0)
    o = jnp.einsum('bhqk,bkhd->bqhd', w, v.astype(jnp.float32))
    surv = rc[..., 0]

    def step(carry, pages):
        o_acc, sv = carry
        kp = cache_k[pages]
        vp = cache_v[pages].astype(jnp.float32)
        zp = jnp.einsum('bqhd,bkhd->bhqk', q, kp).astype(jnp.float32) * SB_SCALE + bh
        lmp = jax.nn.log_sigmoid(-zp)
        rcp = lax.cumsum(lmp, axis=3, reverse=True)
        wp = jnp.exp(jax.nn.log_sigmoid(zp) + rcp - lmp + sv[..., None])
        o_acc = o_acc + jnp.einsum('bhqk,bkhd->bqhd', wp, vp)
        return (o_acc, sv + rcp[..., 0]), None

    (o, _), _ = lax.scan(step, (o, surv), page_table.T, reverse=True)
    return o.reshape(bsz, t, h * d).astype(q.dtype)

def _layer(x, c, attn_fn, lru_conv_prev, lru_h0, ffn_conv_prev, reset_first,
           w_ada, b_ada, g_norm1, w_in, g_q, g_k, b_sb, w_lru_conv, b_lru_conv,
           w_lru_a, b_lru_a, w_lru_x, b_lru_x, lru_lambda, w_out,
           g_norm2, w_up, w_ffn_conv, b_ffn_conv, w_down):
    bsz, t, _ = x.shape
    mod = (jax.nn.silu(c) @ w_ada + b_ada).reshape(bsz, N_MOD, 1, D_MODEL)
    sh1, sc1, gt1, sh2, sc2, gt2 = (mod[:, 0], mod[:, 1], mod[:, 2], mod[:, 3], mod[:, 4], mod[:, 5])

    hn = _rmsnorm(x, g_norm1) * (1.0 + sc1) + sh1
    proj = hn @ w_in
    q, k, v, xl, gl = jnp.split(proj, [ATTN_WIDTH, 2 * ATTN_WIDTH, 3 * ATTN_WIDTH, 3 * ATTN_WIDTH + LRU_WIDTH], axis=-1)
    q = _rmsnorm(q.reshape(bsz, t, N_HEADS, HEAD_DIM), g_q)
    k = _rmsnorm(k.reshape(bsz, t, N_HEADS, HEAD_DIM), g_k)
    v = v.reshape(bsz, t, N_HEADS, HEAD_DIM)
    attn = attn_fn(q, k, v, b_sb)

    xc, lru_conv_new = _causal_dwconv(xl, lru_conv_prev, w_lru_conv, b_lru_conv)
    hl, lru_h_new = _rglru(xc, lru_h0, w_lru_a, b_lru_a, w_lru_x, b_lru_x, lru_lambda, reset_first)
    lru = hl.astype(x.dtype) * jax.nn.gelu(gl)

    mix = jnp.concatenate([attn.astype(x.dtype), lru], axis=-1) @ w_out
    x = x + gt1 * mix

    hn2 = _rmsnorm(x, g_norm2) * (1.0 + sc2) + sh2
    u = hn2 @ w_up
    uc, ffn_conv_new = _causal_dwconv(u, ffn_conv_prev, w_ffn_conv, b_ffn_conv)
    ug, uv = jnp.split(uc, 2, axis=-1)
    x = x + gt2 * ((jax.nn.gelu(ug) * uv) @ w_down)
    return x, k, v, lru_conv_new, lru_h_new.astype(x.dtype), ffn_conv_new

def setup_inputs(seed: int = 0) -> dict:
    key = jax.random.key(seed)
    ks = jax.random.split(key, 32)
    n_pages = PAST_LEN // PAGE_SIZE
    n_used = DEC_BATCH * n_pages
    n_pool = n_used + max(1, n_used // 4)

    def nrm(k, shape, scale):
        return jax.random.normal(k, shape, jnp.float32) * scale

    a0 = jax.random.uniform(ks[20], (DEPTH, LRU_WIDTH), jnp.float32, minval=0.9, maxval=0.999)
    a1 = a0 ** (1.0 / LRU_C)
    return {
        'x_prompt': nrm(ks[0], (BATCH, SEQ, D_MODEL), 1.0),
        'x_sample': nrm(ks[1], (DEC_BATCH, DEC_SEQ, D_MODEL), 1.0),
        'c_prompt': nrm(ks[2], (BATCH, D_MODEL), 1.0),
        'c_sample': nrm(ks[3], (DEC_BATCH, D_MODEL), 1.0),
        'cache_k': nrm(ks[4], (DEPTH, n_pool, PAGE_SIZE, N_HEADS, HEAD_DIM), 1.0),
        'cache_v': nrm(ks[5], (DEPTH, n_pool, PAGE_SIZE, N_HEADS, HEAD_DIM), 1.0),
        'page_table': jax.random.permutation(ks[6], n_pool)[:n_used].reshape(DEC_BATCH, n_pages).astype(jnp.int32),
        'state_lru_conv': nrm(ks[7], (DEPTH, DEC_BATCH, LRU_CONV_W - 1, LRU_WIDTH), 1.0),
        'state_lru_h': nrm(ks[8], (DEPTH, DEC_BATCH, LRU_WIDTH), 0.3),
        'state_ffn_conv': nrm(ks[9], (DEPTH, DEC_BATCH, FFN_CONV_W - 1, 2 * D_FF), 1.0),
        'w_ada': nrm(ks[10], (DEPTH, D_MODEL, N_MOD * D_MODEL), 0.5 * D_MODEL ** -0.5),
        'b_ada': nrm(ks[11], (DEPTH, N_MOD * D_MODEL), 0.02),
        'g_norm1': 1.0 + nrm(ks[12], (DEPTH, D_MODEL), 0.02),
        'w_in': nrm(ks[13], (DEPTH, D_MODEL, N_IN), D_MODEL ** -0.5),
        'g_q': 1.0 + nrm(ks[14], (DEPTH, HEAD_DIM), 0.02),
        'g_k': 1.0 + nrm(ks[15], (DEPTH, HEAD_DIM), 0.02),
        'b_sb': SB_BIAS_INIT + nrm(ks[29], (DEPTH, N_HEADS), 0.1),
        'w_lru_conv': nrm(ks[16], (DEPTH, LRU_CONV_W, LRU_WIDTH), LRU_CONV_W ** -0.5),
        'b_lru_conv': nrm(ks[17], (DEPTH, LRU_WIDTH), 0.02),
        'w_lru_a': nrm(ks[18], (DEPTH, LRU_BLOCKS, LRU_BLOCK_W, LRU_BLOCK_W), LRU_BLOCK_W ** -0.5),
        'b_lru_a': nrm(ks[19], (DEPTH, LRU_BLOCKS, LRU_BLOCK_W), 0.02),
        'w_lru_x': nrm(ks[21], (DEPTH, LRU_BLOCKS, LRU_BLOCK_W, LRU_BLOCK_W), LRU_BLOCK_W ** -0.5),
        'b_lru_x': nrm(ks[22], (DEPTH, LRU_BLOCKS, LRU_BLOCK_W), 0.02),
        'lru_lambda': jnp.log(a1) - jnp.log1p(-a1),
        'w_out': nrm(ks[23], (DEPTH, D_MODEL, D_MODEL), D_MODEL ** -0.5),
        'g_norm2': 1.0 + nrm(ks[24], (DEPTH, D_MODEL), 0.02),
        'w_up': nrm(ks[25], (DEPTH, D_MODEL, 2 * D_FF), D_MODEL ** -0.5),
        'w_ffn_conv': nrm(ks[26], (DEPTH, FFN_CONV_W, 2 * D_FF), FFN_CONV_W ** -0.5),
        'b_ffn_conv': nrm(ks[27], (DEPTH, 2 * D_FF), 0.02),
        'w_down': nrm(ks[28], (DEPTH, D_FF, D_MODEL), D_FF ** -0.5),
    }

def reference(x_prompt, x_sample, c_prompt, c_sample, cache_k, cache_v, page_table,
              state_lru_conv, state_lru_h, state_ffn_conv,
              w_ada, b_ada, g_norm1, w_in, g_q, g_k, b_sb, w_lru_conv, b_lru_conv,
              w_lru_a, b_lru_a, w_lru_x, b_lru_x, lru_lambda, w_out,
              g_norm2, w_up, w_ffn_conv, b_ffn_conv, w_down):
    xp = x_prompt
    xs = x_sample
    kp_l, vp_l, ks_l, vs_l = [], [], [], []
    lcp_l, lcs_l, lhp_l, lhs_l, fcp_l, fcs_l = [], [], [], [], [], []
    for l in range(DEPTH):
        params = (w_ada[l], b_ada[l], g_norm1[l], w_in[l], g_q[l], g_k[l], b_sb[l], w_lru_conv[l], b_lru_conv[l],
                  w_lru_a[l], b_lru_a[l], w_lru_x[l], b_lru_x[l], lru_lambda[l], w_out[l],
                  g_norm2[l], w_up[l], w_ffn_conv[l], b_ffn_conv[l], w_down[l])
        zc = jnp.zeros((xp.shape[0], LRU_CONV_W - 1, LRU_WIDTH), xp.dtype)
        zh = jnp.zeros((xp.shape[0], LRU_WIDTH), xp.dtype)
        zf = jnp.zeros((xp.shape[0], FFN_CONV_W - 1, 2 * D_FF), xp.dtype)
        xp, kp, vp, lcp, lhp, fcp = _layer(xp, c_prompt, _sb_prompt, zc, zh, zf, True, *params)
        bp, sp = kp.shape[0], kp.shape[1]
        kp_l.append(kp.reshape(bp, sp // PAGE_SIZE, PAGE_SIZE, N_HEADS, HEAD_DIM))
        vp_l.append(vp.reshape(bp, sp // PAGE_SIZE, PAGE_SIZE, N_HEADS, HEAD_DIM))
        lcp_l.append(lcp)
        lhp_l.append(lhp)
        fcp_l.append(fcp)
        ck = cache_k[l]
        cv = cache_v[l]
        sample_attn = lambda q, k, v, bias: _sb_sample(q, k, v, bias, ck, cv, page_table)
        xs, ksm, vsm, lcs, lhs, fcs = _layer(xs, c_sample, sample_attn, state_lru_conv[l], state_lru_h[l],
                                             state_ffn_conv[l], False, *params)
        ks_l.append(ksm)
        vs_l.append(vsm)
        lcs_l.append(lcs)
        lhs_l.append(lhs)
        fcs_l.append(fcs)
    return (xp, xs, jnp.stack(kp_l), jnp.stack(vp_l), jnp.stack(ks_l), jnp.stack(vs_l),
            jnp.stack(lcp_l), jnp.stack(lcs_l), jnp.stack(lhp_l), jnp.stack(lhs_l),
            jnp.stack(fcp_l), jnp.stack(fcs_l))


_drawn_inputs = setup_inputs


def setup_inputs(seed=0):
    import zlib

    import numpy as np

    out = dict(_drawn_inputs(seed))
    spreads = {}
    factors = {'cache_k': 3.008,
     'g_norm1': 2.974,
     'g_q': 8.0,
     'g_k': 2.804,
     'b_sb': 8.0,
     'b_lru_a': 8.0,
     'b_lru_x': 6.319,
     'g_norm2': 2.949,
     'b_ffn_conv': 8.0}
    for name, (base, spread) in spreads.items():
        noise = np.random.default_rng([zlib.crc32(name.encode()), seed]).standard_normal(out[name].shape)
        drawn = base * np.exp(spread * noise) if base else spread * noise
        out[name] = jnp.asarray(drawn.astype(out[name].dtype))
    for name, factor in factors.items():
        out[name] = (out[name] * factor).astype(out[name].dtype)
    return out
```

```python
from contextlib import ExitStack

import concourse.bass as bass
from concourse import mybir

F32 = mybir.dt.float32
F32R = mybir.dt.float32r
I32 = mybir.dt.int32
ALU = mybir.AluOpType
ACT = mybir.ActivationFunctionType

P = 128
D = 2048
KT = D // P
SEQ = 512
NB = 8
NS = 8
SAMP = NB * NS
T = SEQ + SAMP
HALF = T // 2
NH = 8
NL = 8
PAGES = 8
KB = 8
SLOTS = 4
NFF = 48
G = 6
NG = NFF // G
NM = 96
CB = 10
EPS = 1e-6
SCALE = float(P) ** -0.5
LRU_C = 8.0

V_BADA, V_G1, V_G2 = 0, 96, 112
V_LCW, V_LCB, V_BA, V_BX, V_LAM, V_GQ, V_GK = 128, 160, 168, 176, 184, 192, 193
V_FCW, V_FCB = 256, 544
B_ADA, B_QKV, B_LRU, B_OUT, B_FFN = 0, 64, 160, 256, 304
J0 = (0, 512, 896, 1152)
QW = (512, 384, 256, 128)
ZB = ((5, 0), (6, 0), (7, 0), (7, 256))


def wait(eng, sem, value):
    if not isinstance(value, int) or value > 0:
        eng.wait_ge(sem, value)


def turns(eng, n, body, straight=1):
    for i in range(straight):
        body(i)
    with eng.Fori(straight, n) as i:
        body(i)


def starts(i):
    return isinstance(i, int) and i == 0


def turn(base, i, per):
    return base + per * i, base // SLOTS + (per // SLOTS) * i


def ffn_up(g, j):
    return B_FFN + 40 * g + 4 * j, B_FFN // SLOTS + 10 * g + j


def ffn_down(g, m):
    return B_FFN + 40 * g + 24 + 4 * m, B_FFN // SLOTS + 10 * g + 6 + m


class Chain:

    def __init__(self, eng, sem):
        self.eng, self.sem, self.start, self.base, self.n = eng, sem, 0, 0, 0

    def enter(self, offset, per):
        self.base, self.per, self.n = offset + self.start, per, 0

    def leave(self):
        assert self.n == self.per, f"{self.n} steps, not {self.per}"

    def advance(self, total):
        self.start += total

    def step(self, ins):
        ins.then_inc(self.sem, 1)
        self.n += 1

    def settle(self):
        self.eng.wait_ge(self.sem, self.base + self.n)

    def link(self, ins):
        self.step(ins)
        self.settle()


def build(nc, x_prompt, x_sample, c_prompt, c_sample, cache_k, cache_v, page_table,
          state_lru_conv, state_lru_h, state_ffn_conv,
          w_ada, b_ada, g_norm1, w_in, g_q, g_k, b_sb, w_lru_conv, b_lru_conv,
          w_lru_a, b_lru_a, w_lru_x, b_lru_x, lru_lambda, w_out,
          g_norm2, w_up, w_ffn_conv, b_ffn_conv, w_down,
          y_prompt, y_sample, k_prompt, v_prompt, k_sample, v_sample,
          lru_conv_prompt, lru_conv_sample, lru_h_prompt, lru_h_sample,
          ffn_conv_prompt, ffn_conv_sample):
    ctx = ExitStack()
    temps = ExitStack()

    def sb(name, shape, dt=F32):
        return ctx.enter_context(nc.sbuf_tensor(name, shape, dt))

    def tmp(name, shape, dt=F32):
        return temps.enter_context(nc.sbuf_tensor(name, shape, dt))

    names = {}

    def sem(name):
        if name not in names:
            names[name] = ctx.enter_context(nc.semaphore(name))
        return names[name]

    x_save = nc.dram_tensor("x_save", (P, KT * T), F32, kind="Internal").ap()

    with ctx:
        act_hi = sb("act_hi", [P, KT, T], F32R)
        act_lo = sb("act_lo", [P, KT, T], F32R)
        X = sb("X", [P, KT, T])
        raw = [sb(f"raw{s}", [P, KB, P]) for s in range(SLOTS)]
        w_hi = [sb(f"w_hi{s}", [P, KB, P], F32R) for s in range(SLOTS)]
        w_lo = [sb(f"w_lo{s}", [P, KB, P], F32R) for s in range(SLOTS)]
        vec = sb("vec", [P, 640])
        mod = sb("mod", [P, NM, CB])
        ident = sb("ident", [P, P])
        neg_later = sb("neg_later", [P, P])
        neg_ones = sb("neg_ones", [P, P])
        before = sb("before", [P, P])
        cs = sb("cs", [P, KT, 2 * CB], F32R)
        eps = sb("eps", [P, 1])
        lst = sb("lst", [P, 256])
        lnew = sb("lnew", [P, 288])
        bias_h = sb("bias_h", [P, NH])
        c8 = sb("c8", [P, 2, NL])
        same = sb("same", [SAMP, SAMP])
        xr = tmp("xr", [P, 5, D])
        vr = tmp("vr", [P, 5, P])
        lsr = tmp("lsr", [P, 2, P])
        sq = tmp("sq", [P, 2, T])
        rs = tmp("rs", [P, T])
        temps.close()
        xr_flat = xr[:].rearrange("p a b -> p (a b)")
        mod_t = xr_flat[:, 0:1024]
        mod_u = xr_flat[:, 1024:2048]
        s1 = xr_flat[:, 2048:2048 + KT * CB].rearrange("p (k c) -> p k c", c=CB)
        hp = [xr_flat[:, 3072 + 512 * i:3584 + 512 * i] for i in range(2)]
        qs = tmp("qs", [P, NH, SAMP])
        vs = tmp("vs", [SAMP, NH, P])
        zs = tmp("zs", [P, NH, SAMP])
        mark = temps.pop_all()
        qraw = tmp("qraw", [P, T])
        kraw = tmp("kraw", [P, T])
        qf = tmp("qf", [P, T])
        kf = tmp("kf", [P, T])
        vf = tmp("vf", [P, T])
        sqq = tmp("sqq", [P, T])
        sqk = tmp("sqk", [P, T])
        zf = tmp("zf", [P, 1280])
        sp_ = tmp("sp_", [P, 1280])
        wt = tmp("wt", [P, 1280])
        vn = tmp("vn", [P, 4, P])
        kn = tmp("kn", [P, 4, P])
        ksn = tmp("ksn", [SAMP, P])
        temps.close()
        kpg = [tmp(f"kpg{i}", [P, NH, P]) for i in range(2)]
        vpg = [tmp(f"vpg{i}", [P, NH, P]) for i in range(2)]
        kt_ = [tmp(f"kt{i}", [P, 4, P]) for i in range(2)]
        bias_z = tmp("bias_z", [P, 512])
        zc = tmp("zc", [P, 512])
        wself = tmp("wself", [SAMP, 512])
        spc = tmp("spc", [P, 512])
        suf = tmp("suf", [P, 512])
        xlp = tmp("xlp", [P, 3 + SEQ + NB * 11])
        xc = tmp("xc", [P, T])
        La = tmp("La", [P, T])
        Lb = tmp("Lb", [P, T])
        Lc = tmp("Lc", [P, T])
        gg = tmp("gg", [P, T])
        wg = tmp("wg", [P, 2, P])
        pt = tmp("pt", [1, 64], I32)
        temps.close()
        mark.close()
        cv = tmp("cv", [P, 18, NM])
        crl = tmp("crl", [P, 3 * P])
        mark2 = temps.pop_all()
        str_ = tmp("str_", [P, 12, P])
        sq2 = tmp("sq2", [P, 2, T])
        xres = tmp("xres", [P, 2, T])
        hp2 = tmp("hp2", [P, 2, SEQ])
        mt2 = tmp("mt2", [P, 2, 1024])
        rs2 = tmp("rs2", [P, T])
        s2 = tmp("s2", [P, KT, CB])
        t64 = tmp("t64", [P, 2, SAMP])
        temps.close()
        g_hi = tmp("g_hi", [P, G, T], F32R)
        g_lo = tmp("g_lo", [P, G, T], F32R)
        up = [tmp(f"up{i}", [P, 2 + SEQ + NB * 10]) for i in range(2)]
        uc = [tmp(f"uc{i}", [P, T]) for i in range(2)]
        gp = tmp("gp", [P, T])
        t64b = tmp("t64b", [P, 2, SAMP])
        temps.close()
        yr = tmp("yr", [P, 2, D])
        crt = tmp("crt", [P, 14, P])
        temps.close()
        mark2.close()

        ps = ctx.enter_context(nc.psum_tensor("ps", [P, 8, 512], F32))
        gps = [ps[:, 0:2, 0:HALF], ps[:, 2:4, 0:HALF]]

        def flat2(a):
            return a.rearrange("p (h n) -> p h n", h=2)

        xlp_s = xlp[:, 3 + SEQ:].rearrange("p (b t) -> p b t", t=11)
        up_s = [u[:, 2 + SEQ:].rearrange("p (b t) -> p b t", t=10) for u in up]

        s_raw = [sem(f"raw_loaded{s}") for s in range(SLOTS)]
        hi_done, lo_done, blk_used = sem("hi_done"), sem("lo_done"), sem("block_used")

        wi_v = w_in[0].rearrange("(k p) n -> p k n", p=P)
        wa_v = w_ada[0].rearrange("(k p) n -> p k n", p=P)
        wo_v = w_out[0].rearrange("(k p) n -> p k n", p=P)
        wu_v = w_up[0].rearrange("(k p) n -> p k n", p=P)
        wd_v = w_down[0].rearrange("(k p) n -> p k n", p=P)

        block = ctx.enter_context(nc.Block())

        @block.sync
        def _(sp):
            def load(u, k, view, row, nk, col):
                wait(sp, lo_done, u[0] + (k - SLOTS + 1))
                sp.dma_start(raw[k % SLOTS][:, 0:nk, :],
                             view[:, bass.ds(row, nk), bass.ds(col, P)]).then_inc(s_raw[k % SLOTS], 16)

            def tile(u, k, view, col):
                for h in range(2):
                    load(u, k + h, view, h * KB, KB, col)

            cflat = X[:].rearrange("p k n -> p (k n)")
            c_loaded = sem("c_loaded")
            sp.wait_ge(sem("zeroed"), 2)
            sp.dma_start(cflat[0:8, 0:D], c_sample).then_inc(c_loaded, 16)
            sp.dma_start(cflat[8:9, 0:D], c_prompt).then_inc(c_loaded, 16)
            vecs = sem("vecs_loaded")

            def rows(t, p0, n, src):
                sp.dma_start(vr[p0:p0 + n, t, :], src).then_inc(vecs, 16)
            rows(0, 0, 96, b_ada.rearrange("a (r c) -> (a r) c", c=P))
            rows(0, 96, 16, g_norm1.rearrange("a (r c) -> (a r) c", c=P))
            rows(0, 112, 16, g_norm2.rearrange("a (r c) -> (a r) c", c=P))
            rows(1, 0, 32, w_lru_conv.rearrange("a w (r c) -> (a w r) c", c=P))
            rows(1, 32, 8, b_lru_conv.rearrange("a (r c) -> (a r) c", c=P))
            rows(1, 40, 8, b_lru_a.rearrange("a r c -> (a r) c"))
            rows(1, 48, 8, b_lru_x.rearrange("a r c -> (a r) c"))
            rows(1, 56, 8, lru_lambda.rearrange("a (r c) -> (a r) c", c=P))
            rows(1, 64, 1, g_q)
            rows(1, 65, 1, g_k)
            fw = w_ffn_conv.rearrange("a w (r c) -> (a w r) c", c=P)
            rows(2, 0, 128, fw[0:128])
            rows(3, 0, 128, fw[128:256])
            rows(4, 0, 32, fw[256:288])
            rows(4, 32, 96, b_ffn_conv.rearrange("a (r c) -> (a r) c", c=P))
            st = state_lru_conv.rearrange("a b w (r c) -> (a b w r) c", c=P)
            sp.dma_start(lsr[:, 0, :], st[0:128]).then_inc(vecs, 16)
            sp.dma_start(lsr[0:64, 1, :], st[128:192]).then_inc(vecs, 16)
            sp.dma_start(lsr[64:128, 1, :], state_lru_h.rearrange("a b (r c) -> (a b r) c", c=P)).then_inc(vecs, 16)
            x_loaded = sem("x_loaded")
            for t in range(4):
                sp.dma_start(xr[:, t, :], x_prompt[0, t * P:(t + 1) * P, :]).then_inc(x_loaded, 16)
            sp.dma_start(xr[0:SAMP, 4, :], x_sample.rearrange("b t d -> (b t) d")).then_inc(x_loaded, 16)

            def ada(i):
                u = turn(B_ADA, i, 8)
                for j in range(4):
                    tile(u, 2 * j, wa_v, 512 * i + 128 * j)
            turns(sp, 8, ada)

            def qkv(i):
                u = turn(B_QKV, i, 12)
                for j in range(3):
                    tile(u, 4 * j, wi_v, 128 * i + 1024 * j)
                    tile(u, 4 * j + 2, wa_v, 384 * i + (32 + j) * 128)
            turns(sp, NH, qkv)

            def lru(i):
                u = turn(B_LRU, i, 12)
                tile(u, 0, wi_v, 128 * i + 3072)
                tile(u, 2, wa_v, 512 * i + 56 * 128)
                tile(u, 4, wa_v, 512 * i + 57 * 128)
                tile(u, 6, wi_v, 128 * i + 4096)
                tile(u, 8, wa_v, 512 * i + 58 * 128)
                tile(u, 10, wa_v, 512 * i + 59 * 128)
            turns(sp, NL, lru)

            def out(i):
                u = turn(B_OUT, i, 12)
                for j in range(4):
                    tile(u, (0, 2, 6, 8)[j], wo_v, 512 * i + 128 * j)
                    if j % 2:
                        tile(u, (4, 10)[j // 2], wa_v, 256 * i + (88 + j // 2) * 128)
            turns(sp, 4, out)

            with sp.Fori(0, NG) as g:
                with sp.Fori(0, G) as j:
                    u = ffn_up(g, j)
                    tile(u, 0, wu_v, 768 * g + 128 * j)
                    tile(u, 2, wu_v, 768 * g + 128 * j + NFF * P)
                with sp.Fori(0, 4) as m:
                    u = ffn_down(g, m)
                    for c in range(4):
                        load(u, c, wd_v, G * g, G, 512 * m + 128 * c)

            for t in range(5):
                sp.wait_ge(sem("y_even"), 2 * t + 2)
                sp.wait_ge(sem("y_odd"), 2 * t + 2)
                dst = y_prompt[0, t * P:(t + 1) * P, :] if t < 4 else y_sample.rearrange("b t d -> (b t) d")
                sp.dma_start(dst, yr[0:P if t < 4 else SAMP, t % 2, :]).then_inc(sem(f"y_stored{t % 2}"), 16)
            sp.wait_ge(sem("y_stored0"), 48)
            sp.wait_ge(sem("y_stored1"), 32)

        @block.tensor
        def _(pe):
            def ready(u, k):
                pe.wait_ge(lo_done, u[0] + (k + 1))

            def product(u, k, out, hi, lo, nk=KB, first=True, last=True, k0=0, each=None):
                ready(u, k)
                s = k % SLOTS
                for kk in range(nk):
                    if each is not None:
                        pe.wait_ge(each, k0 + kk + 1)
                    for w, xs in ((w_hi, (hi, lo)), (w_lo, (hi,))):
                        for x in xs:
                            for h in range(2):
                                mm = pe.matmul(out[:, h, :], w[s][:, kk, :], x[:, k0 + kk, h * HALF:(h + 1) * HALF],
                                               start=first and kk == 0 and w is w_hi and x is hi,
                                               stop=last and kk == nk - 1 and w is w_lo)
                mm.then_inc(blk_used, 1)
                return mm

            def ada_chunk(u, k, j):
                for h in range(2):
                    ready(u, k + h)
                    s = (k + h) % SLOTS
                    for kk in range(KB):
                        for w in (w_hi, w_lo):
                            mm = pe.matmul(ps[:, 4, 20 * j:20 * j + 20], w[s][:, kk, :], cs[:, h * KB + kk, :],
                                           start=h == 0 and kk == 0 and w is w_hi,
                                           stop=h == 1 and kk == KB - 1 and w is w_lo)
                    mm.then_inc(blk_used, 1)

            pe.wait_ge(sem("consts"), 1)
            pe.wait_ge(sem("silu"), 1)
            cflat = X[:].rearrange("p k n -> p (k n)")
            for k in range(KT):
                mm = pe.transpose(ps[:, 0, CB * k:CB * k + CB], cflat[0:CB, D + k * P:D + (k + 1) * P], ident[0:CB, 0:CB])
            mm.then_inc(sem("c_turned"), 1)
            pe.wait_ge(sem("vecs_loaded"), 16 * 17)
            pe.wait_ge(sem("zeroed"), 2)
            for t in range(5):
                pe.transpose(ps[:, 1 + t // 4, (t % 4) * P:(t % 4 + 1) * P], vr[:, t, :], ident[:])
            for t in range(2):
                mm = pe.transpose(ps[:, 3, t * P:(t + 1) * P], lsr[:, t, :], ident[:])
            mm.then_inc(sem("vecs_turned"), 1)
            pe.wait_ge(sem("x_loaded"), 80)
            pe.wait_ge(sem("c_taken"), 1)
            pe.wait_ge(sem("vecs_taken"), 3)
            XB = ((5, 7), (6, 3))

            def squares(k, first, last, ready_sem):
                pe.wait_ge(ready_sem, k + 1)
                for h in range(2):
                    mm = pe.matmul(ps[:, 1 + h, 0:HALF], neg_ones[:], sq[:, k % 2, h * HALF:(h + 1) * HALF],
                                   start=first, stop=last)
                mm.then_inc(sem("squares_used"), 1)

            for k in range(KT):
                if k >= 2:
                    pe.wait_ge(sem("x_taken_p"), k - 1)
                    pe.wait_ge(sem("x_taken_s"), k - 1)
                bp, bs = XB[k % 2]
                for t in range(4):
                    pe.transpose(ps[:, bp, t * P:(t + 1) * P], xr[:, t, k * P:(k + 1) * P], ident[:])
                pe.transpose(ps[:, bs, 0:SAMP], xr[0:SAMP, 4, k * P:(k + 1) * P], ident[0:SAMP, 0:SAMP]).then_inc(sem("x_turned"), 1)
                if k:
                    squares(k - 1, k == 1, False, sem("sq_ready"))
            squares(KT - 1, False, True, sem("sq_ready"))

            for kk in (KT - 1,):
                pe.wait_ge(sem("x_taken_p"), kk + 1)
                pe.wait_ge(sem("x_taken_s"), kk + 1)

            def ada(i):
                u = turn(B_ADA, i, 8)
                wait(pe, sem("bank4_taken"), i)
                for j in range(4):
                    ada_chunk(u, 2 * j, j)
            turns(pe, 8, ada)

            def scores(i):
                pe.wait_ge(sem("qk_ready"), i)
                pe.wait_ge(sem("rk_taken"), i)
                wait(pe, sem("o_taken"), i - 1)
                for j in range(4):
                    b, c = ZB[j]
                    pe.matmul(ps[:, b, c:c + QW[j]], kf[:, j * P:(j + 1) * P], qf[:, j * P:SEQ], start=True, stop=True)
                pe.matmul(ps[0:SAMP, 4, 384:384 + SAMP], kf[:, SEQ:T], qf[:, SEQ:T], start=True, stop=True) \
                  .then_inc(sem("scores_mm"), 1)

            def sums(i):
                pe.wait_ge(sem("sp_ready"), i)
                for j in range(4):
                    b, c = ZB[j]
                    mm = pe.matmul(ps[:, b, c:c + QW[j]], neg_later[:], sp_[:, J0[j]:J0[j] + QW[j]],
                                   start=True, stop=j == 3)
                    for jj in range(j + 1, 4):
                        c2 = c + (jj - j) * P
                        mm = pe.matmul(ps[:, b, c2:c2 + QW[jj]], neg_ones[:], sp_[:, J0[jj]:J0[jj] + QW[jj]],
                                       start=False, stop=jj == 3)
                mm.then_inc(sem("sums_mm"), 1)

            def turn_kv(i):
                for t in range(4):
                    pe.transpose(ps[:, 2, t * P:(t + 1) * P], vf[:, t * P:(t + 1) * P], ident[:])
                for t in range(4):
                    pe.transpose(ps[:, 3, t * P:(t + 1) * P], kf[:, t * P:(t + 1) * P], ident[:])
                pe.transpose(ps[0:SAMP, 4, 128:256], vf[:, SEQ:T], ident[:])
                pe.transpose(ps[0:SAMP, 4, 256:384], kf[:, SEQ:T], ident[:]).then_inc(sem("kv_turned"), 1)

            def weigh(i):
                pe.wait_ge(sem("w_ready"), i)
                pe.wait_ge(sem("vn_taken"), i)
                for j in range(4):
                    mm = pe.matmul(ps[:, 7, j * P:SEQ], vn[:, j, :], wt[:, J0[j]:J0[j] + QW[j]],
                                   start=j == 0, stop=j == 3)
                mm.then_inc(sem("o_mm"), 1)

            def head_squares(b0, src, out_sem):
                for h in range(2):
                    mm = pe.matmul(ps[:, b0 + h, 0:HALF], neg_ones[:], src[:, h * HALF:(h + 1) * HALF],
                                   start=True, stop=True)
                mm.then_inc(out_sem, 1)

            def qkv(i):
                u = turn(B_QKV, i, 12)
                first = starts(i)
                wait(pe, sem("v_out"), i)
                each = sem("x1_ready") if first else None
                product(u, 0, gps[0], act_hi, act_lo, last=False, each=each)
                product(u, 1, gps[0], act_hi, act_lo, first=False, k0=KB, each=each)
                pe.wait_ge(sem("bank4_taken"), i + 8)
                ada_chunk(u, 2, 0)
                if not first:
                    scores(i)
                wait(pe, sem("rq_taken"), i)
                product(u, 4, gps[1], act_hi, act_lo, last=False)
                product(u, 5, gps[1], act_hi, act_lo, first=False, k0=KB)
                ada_chunk(u, 6, 1)
                if not first:
                    sums(i)
                pe.wait_ge(sem("q_out"), 2 * i + 2)
                product(u, 8, gps[0], act_hi, act_lo, last=False)
                pe.wait_ge(sem("k_out"), 2 * i + 2)
                if not first:
                    turn_kv(i)
                product(u, 9, gps[0], act_hi, act_lo, first=False, k0=KB)
                ada_chunk(u, 10, 2)
                if not first:
                    weigh(i)
                    pe.wait_ge(sem("kn_taken"), i)
                head_squares(2, sqq, sem("ssq_mm"))
                head_squares(5, sqk, sem("ssk_mm"))
            turns(pe, NH, qkv, 2)

            pe.wait_ge(sem("bank4_taken"), 16)
            pe.wait_ge(sem("rq_taken"), NH)
            scores(NH)
            sums(NH)
            turn_kv(NH)
            weigh(NH)
            pe.wait_ge(sem("o_taken"), NH)
            pe.wait_ge(sem("self_sp_ready"), 1)
            pe.matmul(ps[0:SAMP, 7, :], neg_later[0:SAMP, 0:SAMP], zs[0:SAMP].rearrange("p h q -> p (h q)"),
                      start=True, stop=True).then_inc(sem("self_mm"), 1)
            pe.wait_ge(sem("self_done"), 1)

            def turn_k(i, s, a):
                if a == 0:
                    pe.wait_ge(sem(f"k_loaded{s % 2}"), 64 * i + 16 * (s // 2 + 1))
                wait(pe, sem(("ka_taken", "kb_taken")[a]), 8 * i + s)
                for h in range(4):
                    mm = pe.transpose(ps[:, 5 + a, h * P:(h + 1) * P], kpg[s % 2][:, 4 * a + h, :], ident[:])
                mm.then_inc(sem(("ka_turned", "kb_turned")[a]), 1)

            def score_k(i, s, a):
                pe.wait_ge(sem(("ka_taken", "kb_taken")[a]), 8 * i + s + 1)
                for h in range(4):
                    c = s * 64 + (4 * a + h) * NS
                    mm = pe.matmul(ps[:, 7, c:c + NS], kt_[a][:, h, :], qs[:, 4 * a + h, bass.ds(8 * i, NS)],
                                   start=True, stop=True)
                mm.then_inc(sem(("ka_used", "kb_used")[a]), 1)

            def pages(i, s0):
                for a in range(2):
                    turn_k(i, s0, a)
                for s in range(s0, s0 + 4):
                    for a in range(2):
                        score_k(i, s, a)
                        if s + 1 < s0 + 4:
                            turn_k(i, s + 1, a)

            def lru(i):
                u = turn(B_LRU, i, 12)
                wait(pe, sem("r_taken"), i)
                product(u, 0, gps[0], act_hi, act_lo, last=False)
                wait(pe, sem("o2_taken"), i)
                pages(i, 0)
                product(u, 1, gps[0], act_hi, act_lo, first=False, k0=KB)
                pe.wait_ge(sem("bank4_taken"), i + 17)
                ada_chunk(u, 2, 0)
                ada_chunk(u, 4, 1)
                pages(i, 4)
                wait(pe, sem("i_taken"), i)
                product(u, 6, gps[1], act_hi, act_lo, last=False)
                pe.wait_ge(sem("spc_ready"), i + 1)
                pe.matmul(ps[:, 7, :], neg_later[:], spc[:], start=True, stop=False)
                pe.matmul(ps[:, 7, :], neg_ones[:], suf[:], start=False, stop=True).then_inc(sem("sums2_mm"), 1)
                product(u, 7, gps[1], act_hi, act_lo, first=False, k0=KB)
                ada_chunk(u, 8, 2)
                ada_chunk(u, 10, 3)
                pe.wait_ge(sem("gates_loaded"), 32 * i + 32)
                pe.wait_ge(sem("xc_ready"), i + 1)
                for h in range(2):
                    mm = pe.matmul(ps[:, h, 0:HALF], wg[:, 0, :], xc[:, h * HALF:(h + 1) * HALF], start=True, stop=True)
                mm.then_inc(sem("r_mm"), 1)
                pe.wait_ge(sem("gl_out"), i + 1)
                for h in range(2):
                    mm = pe.matmul(ps[:, 2 + h, 0:HALF], wg[:, 1, :], xc[:, h * HALF:(h + 1) * HALF], start=True, stop=True)
                mm.then_inc(sem("i_mm"), 1)
                pe.wait_ge(sem("wc_ready"), i + 1)
                for s in range(PAGES):
                    pe.wait_ge(sem(f"v_loaded{s % 2}"), 64 * i + 16 * (s // 2 + 1))
                    for h in range(NH):
                        mm = pe.matmul(ps[:, 7, h * NS:(h + 1) * NS], vpg[s % 2][:, h, :],
                                       suf[:, s * 64 + h * NS:s * 64 + (h + 1) * NS],
                                       start=s == 0 and h == 0, stop=False, skip_group_check=True)
                    mm.then_inc(sem("v_used"), 1)
                for h in range(NH):
                    mm = pe.matmul(ps[:, 7, h * NS:(h + 1) * NS], vs[:, h, :],
                                   wself[:, bass.ds(8 * i + h * SAMP, NS)],
                                   start=False, stop=True, skip_group_check=True)
                mm.then_inc(sem("o2_mm"), 1)
            turns(pe, NL, lru)

            def sum2(m, slot, first, last):
                pe.wait_ge(sem("sq2_ready"), m + 1)
                for h in range(2):
                    mm = pe.matmul(ps[:, 5 + h, 0:HALF], neg_ones[:], sq2[:, slot, h * HALF:(h + 1) * HALF],
                                   start=first, stop=last)
                mm.then_inc(sem("sq2_used"), 1)

            def out(i):
                u = turn(B_OUT, i, 12)
                first = isinstance(i, int)
                for j in range(4):
                    wait(pe, sem("x2_ready"), 4 * i + (j - 1))
                    if first and j == 0:
                        pe.wait_ge(sem("r_taken"), NL)
                    if first and j == 1:
                        pe.wait_ge(sem("i_taken"), NL)
                    k = (0, 2, 6, 8)[j]
                    each = sem("mix_ready") if first and j == 0 else None
                    product(u, k, gps[j % 2], act_hi, act_lo, last=False, each=each)
                    product(u, k + 1, gps[j % 2], act_hi, act_lo, first=False, k0=KB, each=each)
                    if j % 2:
                        if j == 1:
                            pe.wait_ge(sem("bank4_taken"), i + 25)
                        ada_chunk(u, k + 2, j // 2)
                    if not first or j:
                        sum2(4 * i + (j - 1), (j + 1) % 2, first and j == 1, False)
            turns(pe, 4, out)
            sum2(KT - 1, 1, False, True)
            pe.wait_ge(sem("ffn_state_loaded"), 16)
            pe.wait_ge(sem("x2_ready"), KT)
            pe.wait_ge(sem("bank4_taken"), 29)
            for t in range(12):
                mm = pe.transpose(ps[:, (7, 4, 3)[t // 4], (t % 4) * P:(t % 4 + 1) * P], str_[:, t, :], ident[:])
            mm.then_inc(sem("ffn_state_turned"), 1)
            for t, n in ((0, P), (1, P), (2, 32)):
                mm = pe.transpose(ps[0:n, 2, t * P:(t + 1) * P], lnew[:, t * P:t * P + n], ident[:])
            mm.then_inc(sem("lnew_turned"), 1)

            def up_tile(g, j, each=None):
                u, nt = ffn_up(g, j), G * g + j
                wait(pe, sem("gate_out"), 3 * nt)
                if not isinstance(g, int) or g:
                    pe.wait_ge(sem("y_taken"), KT * g)
                product(u, 0, gps[0], act_hi, act_lo, last=False, each=each)
                product(u, 1, gps[0], act_hi, act_lo, first=False, k0=KB, each=each)
                if each is not None:
                    pe.wait_ge(sem("cv_taken"), 3)
                    pe.wait_ge(sem("lnew_taken"), 2)
                wait(pe, sem("value_out"), 3 * nt)
                product(u, 2, gps[1], act_hi, act_lo, last=False)
                product(u, 3, gps[1], act_hi, act_lo, first=False, k0=KB)

            def down(g):
                pe.wait_ge(sem("gate_out"), 3 * G * g + 3 * G)
                pe.wait_ge(sem("value_out"), 3 * G * g + 3 * G)
                pe.wait_ge(sem("g_ready"), G * g + G)

                def four(m):
                    u = ffn_down(g, m)
                    for c in range(4):
                        if not isinstance(m, int) or m or c >= 2:
                            pe.wait_ge(sem("y_taken"), KT * g + 4 * m + c - 1)
                        product(u, c, gps[c % 2], g_hi, g_lo, nk=G)
                four(0)
                with pe.Fori(1, 4) as m:
                    four(m)

            up_tile(0, 0, each=sem("x3_ready"))
            with pe.Fori(1, G) as j:
                up_tile(0, j)
            down(0)
            with pe.Fori(1, NG) as g:
                with pe.Fori(0, G) as j:
                    up_tile(g, j)
                down(g)

            pe.wait_ge(sem("y_taken"), KT * NG)
            pe.wait_ge(sem("cv_saved"), 4 * NFF)
            n = 0
            for t in range(5):
                w = P if t < 4 else SAMP
                for q in range(4):
                    if n >= 8:
                        pe.wait_ge(sem("y_odd" if n % 2 else "y_even"), (n - 8) // 2 + 1)
                    for k in range(4):
                        mm = pe.transpose(ps[0:w, n % 8, k * P:(k + 1) * P], X[:, 4 * q + k, t * P:t * P + w], ident[:])
                    mm.then_inc(sem("y_turned"), 1)
                    n += 1
            cvf = cv[:].rearrange("p r m -> p (r m)")
            for q in range(4):
                pe.wait_ge(sem("y_odd" if n % 2 else "y_even"), (n - 8) // 2 + 1)
                for k in range(4):
                    t = 4 * q + k
                    if t < 14:
                        w = min(P, 18 * NM - t * P)
                        mm = pe.transpose(ps[0:w, n % 8, k * P:(k + 1) * P], cvf[:, t * P:t * P + w], ident[:])
                mm.then_inc(sem("y_turned"), 1)
                n += 1

        @block.scalar
        def _(act):
            ch = Chain(act, sem("act_steps"))

            def hi(u, k):
                s = k % SLOTS
                wait(act, blk_used, u[0] + (k - SLOTS + 1))
                act.wait_ge(s_raw[s], 16 * u[1] + 16 * (k // SLOTS + 1))
                act.activation(w_hi[s][:], raw[s][:], ACT.Copy).then_inc(hi_done, 1)

            def used(u, k):
                act.wait_ge(blk_used, u[0] + k)

            act.wait_ge(sem("c_loaded"), 32)
            cflat = X[:].rearrange("p k n -> p (k n)")
            act.activation(cflat[0:CB, D:2 * D], cflat[0:CB, 0:D], ACT.Silu).then_inc(sem("silu"), 1)
            act.wait_ge(sem("c_turned"), 1)
            act.activation(cs[:, :, 0:CB], ps[:, 0, 0:KT * CB].rearrange("p (k c) -> p k c", c=CB), ACT.Copy) \
               .then_inc(sem("c_hi"), 1)
            act.wait_ge(sem("vecs_turned"), 1)
            act.activation(vec[:, 0:512], ps[:, 1, :], ACT.Copy).then_inc(sem("vecs_taken"), 1)
            act.activation(vec[:, 512:640], ps[:, 2, 0:P], ACT.Copy).then_inc(sem("vecs_taken"), 1)
            u = turn(B_ADA, 0, 8)
            for k in range(SLOTS):
                hi(u, k)
            act.wait_ge(sem("c_taken"), 1)
            for k in range(KT):
                act.wait_ge(sem("x_turned"), k + 1)
                act.activation(X[:, k, 0:SEQ], ps[:, 5 + k % 2, :], ACT.Copy).then_inc(sem("x_taken_p"), 1)
                act.wait_ge(sem("x_taken_p"), k + 1)
                act.wait_ge(sem("x_taken_s"), k + 1)
                if k >= 2:
                    act.wait_ge(sem("squares_used"), k - 1)
                act.activation(sq[:, k % 2, :], X[:, k, :], ACT.Square).then_inc(sem("sq_ready"), 1)
            act.dma_start(x_save, X[:].rearrange("p k n -> p (k n)")).then_inc(sem("x_saved"), 16)
            act.wait_ge(sem("squares_used"), KT)
            ch.enter(0, 1)
            ch.link(act.activation(flat2(rs[:]), ps[:, 1:3, 0:HALF], ACT.Ln, bias=eps[:], scale=-1.0 / D))
            act.activation(rs[:], rs[:], ACT.Exp, scale=-0.5).then_inc(sem("rs_ready"), 1)
            ch.advance(1)

            def ada(i):
                u = turn(B_ADA, i, 8)
                for k in range(8):
                    hi(u, k + SLOTS)
            turns(act, 8, ada)

            for k in range(KT):
                act.wait_ge(sem("hp_ready"), k + 1)
                act.activation(act_hi[:, k, 0:SEQ], hp[k % 2], ACT.Identity, bias=mod[:, k, 8:9]).then_inc(sem("x1_hi"), 1)
                if k == 0:
                    act.wait_ge(sem("hs_ready"), 1)
                    act.activation(act_hi[:, :, SEQ:T], mod_t.rearrange("p (k n) -> p k n", n=SAMP), ACT.Copy) \
                       .then_inc(sem("x1_hi_s"), 1)

            act.wait_ge(sem("vecs_taken"), 3)
            act.wait_ge(sem("x_saved"), 16)
            def softplus_part(i):
                act.wait_ge(sem("z_taken"), i)
                ch.link(act.activation(wt[:], zf[:], ACT.Abs))
                ch.link(act.activation(wt[:], wt[:], ACT.Exp, scale=-1.0))
                act.activation(wt[:], wt[:], ACT.Ln, bias=1.0).then_inc(sem("lz_ready"), 1)

            def weights(i):
                act.wait_ge(sem("arg_ready"), i)
                act.activation(wt[:], zf[:], ACT.Exp).then_inc(sem("w_exp"), 1)

            def take_v(i):
                act.wait_ge(sem("kv_turned"), i)
                wait(act, sem("o_mm"), i - 1)
                wait(act, sem("v_stored"), 16 * i - 16)
                act.activation(vn[:], ps[:, 2, :].rearrange("p (t d) -> p t d", d=P), ACT.Copy).then_inc(sem("vn_taken"), 1)

            def take_o(i):
                act.wait_ge(sem("o_mm"), i)
                act.activation(X[:, bass.ds(i - 1, 1), 0:SEQ].rearrange("p a n -> p (a n)"), ps[:, 7, :], ACT.Copy).then_inc(sem("o_taken"), 1)

            def qkv(i):
                u, prev = turn(B_QKV, i, 12), not starts(i)
                hi(u, 4)
                hi(u, 5)
                used(u, 2)
                wait(act, sem("qk_ready"), i)
                act.activation(flat2(sqq[:]), gps[0], ACT.Square).then_inc(sem("q_out"), 1)
                act.activation(flat2(qraw[:]), gps[0], ACT.Copy).then_inc(sem("q_out"), 1)
                hi(u, 6)
                hi(u, 7)
                if prev:
                    ch.enter(2 * i - 2, 2)
                    softplus_part(i)
                    ch.leave()
                hi(u, 8)
                hi(u, 9)
                used(u, 6)
                act.activation(flat2(sqk[:]), gps[1], ACT.Square).then_inc(sem("k_out"), 1)
                act.activation(flat2(kraw[:]), gps[1], ACT.Copy).then_inc(sem("k_out"), 1)
                hi(u, 10)
                hi(u, 11)
                if prev:
                    weights(i)
                hi(u, 12)
                if prev:
                    take_v(i)
                hi(u, 13)
                used(u, 10)
                act.activation(flat2(vf[:]), gps[0], ACT.Copy).then_inc(sem("v_out"), 1)
                hi(u, 14)
                hi(u, 15)
                if prev:
                    take_o(i)
                for src, b0, mm, rd, done in ((sqq, 2, "ssq_mm", "rq_taken", "rq_ready"),
                                              (sqk, 5, "ssk_mm", "rk_taken", "rk_ready")):
                    act.wait_ge(sem(mm), i + 1)
                    act.activation(flat2(src[:]), ps[:, b0:b0 + 2, 0:HALF], ACT.Ln, bias=eps[:], scale=-1.0 / P) \
                       .then_inc(sem(rd), 1)
                    act.wait_ge(sem(rd), i + 1)
                    act.activation(src[:], src[:], ACT.Exp, scale=-0.5).then_inc(sem(done), 1)
            turns(act, NH, qkv, 2)
            ch.advance(2 * NH - 2)
            ch.enter(0, 2)
            softplus_part(NH)
            ch.leave()
            ch.advance(2)
            weights(NH)
            take_v(NH)
            take_o(NH)

            zsf = zs[0:SAMP].rearrange("p h q -> p (h q)")
            ch.enter(0, 5)
            act.wait_ge(sem("self_z"), 1)
            ch.link(act.activation(wself[:], zsf, ACT.Abs))
            ch.link(act.activation(wself[:], wself[:], ACT.Exp, scale=-1.0))
            act.activation(wself[:], wself[:], ACT.Ln, bias=1.0).then_inc(sem("self_l"), 1)
            act.wait_ge(sem("self_arg"), 1)
            act.activation(wself[:], spc[0:SAMP, :], ACT.Exp).then_inc(sem("self_w"), 1)
            lam = vec[:, V_LAM:V_LAM + NL]
            ch.link(act.activation(c8[:, 0, :], lam, ACT.Abs))
            ch.link(act.activation(c8[:, 0, :], c8[:, 0, :], ACT.Exp, scale=-1.0))
            ch.link(act.activation(c8[:, 0, :], c8[:, 0, :], ACT.Ln, bias=1.0))
            ch.leave()
            ch.advance(5)
            act.activation(c8[:, 1, :], lam, ACT.Relu, scale=-1.0).then_inc(sem("c8_parts"), 1)

            def recurrence(i):
                act.wait_ge(sem("c8_ready"), 1)
                act.wait_ge(sem("r_taken"), i)
                act.wait_ge(sem("lnew_saved"), 2 * i)
                act.wait_ge(sem("xc_ready"), i)
                act.activation(Lc[:], La[:], ACT.Exp, scale=c8[:, 0, bass.ds(i - 1, 1)]).then_inc(sem("a_ready"), 1)
                act.activation(xlp[:, 3:3 + T], La[:], ACT.Tanh, scale=c8[:, 1, bass.ds(i - 1, 1)]).then_inc(sem("a_ready"), 1)
                act.wait_ge(sem("m2_ready"), i)
                act.activation(xlp[:, 3:3 + T], xlp[:, 3:3 + T], ACT.Sqrt).then_inc(sem("m_ready"), 1)

            def take_keys(i, s):
                act.wait_ge(sem("ka_turned"), 8 * i + (s + 1))
                wait(act, sem("ka_used"), 8 * i + s)
                act.activation(kt_[0][:], ps[:, 5, :].rearrange("p (h k) -> p h k", k=P), ACT.Copy).then_inc(sem("ka_taken"), 1)

            def lru(i):
                u = turn(B_LRU, i, 12)
                if not isinstance(i, int):
                    recurrence(i)
                    ch.enter(2 * i, 2)
                else:
                    ch.enter(0, 2)
                hi(u, 4)
                for s in range(4):
                    take_keys(i, s)
                hi(u, 5)
                used(u, 2)
                wait(act, sem("lru_done"), i)
                act.activation(xlp[:, 3:3 + HALF], ps[:, 0, 0:HALF], ACT.Copy).then_inc(sem("xl_out"), 1)
                act.activation(xlp[:, 3 + HALF:3 + SEQ], ps[:, 1, 0:SEQ - HALF], ACT.Copy).then_inc(sem("xl_out"), 1)
                act.activation(xlp_s[:, :, 3:11], ps[:, 1, SEQ - HALF:HALF].rearrange("p (b t) -> p b t", t=NS), ACT.Copy) \
                   .then_inc(sem("xl_out"), 1)
                for k in range(6, 10):
                    hi(u, k)
                for s in range(4, 8):
                    take_keys(i, s)
                act.wait_ge(sem("zc_taken"), i + 1)
                ch.link(act.activation(spc[:], zc[:], ACT.Abs))
                ch.link(act.activation(spc[:], spc[:], ACT.Exp, scale=-1.0))
                act.activation(spc[:], spc[:], ACT.Ln, bias=1.0).then_inc(sem("lc_ready"), 1)
                ch.leave()
                hi(u, 10)
                act.wait_ge(sem("argc_ready"), i + 1)
                act.activation(suf[:], zc[:], ACT.Exp).then_inc(sem("wc_ready"), 1)
                hi(u, 11)
                used(u, 8)
                act.activation(flat2(gg[:]), gps[1], ACT.Gelu_apprx_tanh).then_inc(sem("gl_out"), 1)
                for k in range(12, 16):
                    hi(u, k)
                act.wait_ge(sem("r_mm"), i + 1)
                act.activation(flat2(La[:]), gps[0], ACT.Sigmoid, bias=vec[:, bass.ds(V_BA + i, 1)]).then_inc(sem("r_taken"), 1)
                act.wait_ge(sem("i_mm"), i + 1)
                act.activation(flat2(Lb[:]), gps[1], ACT.Sigmoid, bias=vec[:, bass.ds(V_BX + i, 1)]).then_inc(sem("i_taken"), 1)
                act.wait_ge(sem("o2_mm"), i + 1)
                act.activation(X[:, 0:NH, bass.ds(SEQ + NS * i, NS)], ps[:, 7, 0:NH * NS].rearrange("p (h q) -> p h q", q=NS),
                               ACT.Copy).then_inc(sem("o2_taken"), 1)
            turns(act, NL, lru)
            ch.advance(2 * NL)
            recurrence(NL)

            act.wait_ge(blk_used, B_OUT)
            act.wait_ge(sem("o_taken"), NH)
            act.wait_ge(sem("o2_taken"), NL)
            for k in range(KT):
                if k == KT - 1:
                    act.wait_ge(sem("lru_done"), NL)
                act.activation(act_hi[:, k, :], X[:, k, :], ACT.Copy).then_inc(sem("mix_hi"), 1)

            def out(i):
                u = turn(B_OUT, i, 12)
                for j in range(4):
                    k = (0, 2, 6, 8)[j]
                    hi(u, k + 4)
                    hi(u, k + 5)
                    if j % 2:
                        hi(u, k + 6)
                        hi(u, k + 7)
                    act.wait_ge(sem("x2_ready"), 4 * i + (j + 1))
                    wait(act, sem("sq2_used"), 4 * i + (j - 1))
                    act.activation(sq2[:, j % 2, :], X[:, bass.ds(4 * i + j, 1), :].rearrange("p a n -> p (a n)"), ACT.Square) \
                       .then_inc(sem("sq2_ready"), 1)
            turns(act, 4, out)
            act.wait_ge(sem("sq2_used"), KT)
            act.activation(flat2(rs2[:]), ps[:, 5:7, 0:HALF], ACT.Ln, bias=eps[:], scale=-1.0 / D).then_inc(sem("rs2_taken"), 1)
            act.wait_ge(sem("rs2_taken"), 1)
            act.activation(rs2[:], rs2[:], ACT.Exp, scale=-0.5).then_inc(sem("rs2_ready"), 1)
            act.wait_ge(sem("ffn_state_turned"), 1)
            for q in range(3):
                act.activation(cv[:].rearrange("p r m -> p (r m)")[:, 2 * NM + 512 * q:2 * NM + 512 * (q + 1)],
                               ps[:, (7, 4, 3)[q], :], ACT.Copy).then_inc(sem("cv_taken"), 1)
            for k in range(KT):
                act.wait_ge(sem("hp2_ready"), k + 1)
                act.activation(act_hi[:, k, 0:SEQ], hp2[:, k % 2, :], ACT.Identity, bias=mod[:, 48 + k, 8:9]).then_inc(sem("x3_hi"), 1)
                if k == 0:
                    act.wait_ge(sem("hs2_ready"), 1)
                    act.activation(act_hi[:, :, SEQ:T], mt2[:, 0, :].rearrange("p (k n) -> p k n", n=SAMP), ACT.Copy) \
                       .then_inc(sem("x3_hi_s"), 1)

            def take_up(u, which, nt, done):
                wait(act, sem("cv_saved"), 4 * nt)
                wait(act, sem("g_ready"), nt)
                b0 = 2 * which
                act.activation(up[which][:, 2:2 + HALF], ps[:, b0, 0:HALF], ACT.Copy).then_inc(done, 1)
                act.activation(up[which][:, 2 + HALF:2 + SEQ], ps[:, b0 + 1, 0:SEQ - HALF], ACT.Copy).then_inc(done, 1)
                act.activation(up_s[which][:, :, 2:10], ps[:, b0 + 1, SEQ - HALF:HALF].rearrange("p (b t) -> p b t", t=NS),
                               ACT.Copy).then_inc(done, 1)

            def up_tile(g, j):
                u, nt = ffn_up(g, j), G * g + j
                hi(u, 4)
                hi(u, 5)
                used(u, 2)
                take_up(u, 0, nt, sem("gate_out"))
                hi(u, 6)
                hi(u, 7)
                used(u, 4)
                take_up(u, 1, nt, sem("value_out"))
                act.wait_ge(sem("gate_conv"), nt + 1)
                act.activation(uc[0][:], uc[0][:], ACT.Gelu_apprx_tanh).then_inc(sem("gelu_done"), 1)
                act.wait_ge(sem("gp_ready"), nt + 1)
                act.activation(g_hi[:, bass.ds(j, 1), :].rearrange("p a n -> p (a n)"), gp[:], ACT.Copy).then_inc(sem("g_hi_ready"), 1)

            def down(g, last):
                def four(m, end=False):
                    u = ffn_down(g, m)
                    if not end:
                        for c in range(4):
                            hi(u, c + 4)
                with act.Fori(0, 3) as m:
                    four(m)
                four(3, last)

            def group(g, last=False):
                if isinstance(g, int) and g == 0:
                    up_tile(0, 0)
                    with act.Fori(1, G) as j:
                        up_tile(0, j)
                else:
                    with act.Fori(0, G) as j:
                        up_tile(g, j)
                down(g, last)
            group(0)
            with act.Fori(1, NG - 1) as g:
                group(g)
            group(NG - 1, True)

            for n in range(0, 24, 2):
                act.wait_ge(sem("y_turned"), n + 1)
                t, q = n // 4, n % 4
                w = P if t != 4 else SAMP
                if t < 5:
                    if t >= 2 and q == 0:
                        act.wait_ge(sem(f"y_stored{t % 2}"), 16 * (t // 2))
                    dst = yr[0:w, t % 2, q * 512:(q + 1) * 512]
                    act.activation(dst, ps[0:w, n % 8, :], ACT.Copy).then_inc(sem("y_even"), 1)
                else:
                    act.activation(crt[:, 4 * q:4 * q + 4, :], ps[:, n % 8, :].rearrange("p (a b) -> p a b", b=P), ACT.Copy).then_inc(sem("y_even"), 1)

        @block.vector
        def _(dve):
            ch = Chain(dve, sem("dve_steps"))

            def lo(u, k):
                s = k % SLOTS
                dve.wait_ge(hi_done, u[0] + (k + 1))
                dve.tensor_tensor(w_lo[s][:], raw[s][:], w_hi[s][:].bitcast(F32), ALU.subtract).then_inc(lo_done, 1)

            def take_mod(u, blocks, n, m0, t, done=True):
                dve.wait_ge(blk_used, u[0] + blocks)
                pm = ps[:, 4, 0:20 * n].rearrange("p (n c) -> p n c", c=20)
                out = mod[:, bass.ds(m0, n), :]
                dve.tensor_tensor(out, pm[:, :, 0:CB], vec[:, bass.ds(m0, n)].unsqueeze(2).to_broadcast([P, n, CB]),
                                  ALU.add).then_inc(sem("mod_part"), 1)
                dve.wait_ge(sem("mod_part"), t + 1)
                ins = dve.tensor_tensor(out, pm[:, :, CB:20], out, ALU.add)
                if done:
                    ins.then_inc(sem("bank4_taken"), 1)

            dve.wait_ge(sem("c_turned"), 1)
            dve.wait_ge(sem("c_hi"), 1)
            dve.tensor_tensor(cs[:, :, CB:2 * CB], ps[:, 0, 0:KT * CB].rearrange("p (k c) -> p k c", c=CB),
                              cs[:, :, 0:CB].bitcast(F32), ALU.subtract).then_inc(sem("c_taken"), 1)
            dve.wait_ge(sem("vecs_turned"), 1)
            dve.tensor_copy(lst[:], ps[:, 3, 0:256]).then_inc(sem("vecs_taken"), 1)
            u = turn(B_ADA, 0, 8)
            for k in range(SLOTS):
                lo(u, k)
            for k in range(KT):
                dve.wait_ge(sem("x_turned"), k + 1)
                dve.tensor_copy(X[:, k, SEQ:T], ps[:, (7, 3)[k % 2], 0:SAMP]).then_inc(sem("x_taken_s"), 1)
            dve.wait_ge(sem("vecs_taken"), 3)
            dve.wait_ge(sem("bias_loaded"), 16)
            dve.wait_ge(sem("consts"), 1)

            def ada(i):
                u = turn(B_ADA, i, 8)
                for k in range(8):
                    lo(u, k + SLOTS)
                take_mod(u, 8, 4, 4 * i, i)
            turns(dve, 8, ada)

            def modulate(s_, t_, v_, rstd, m_scale, m_shift, v_g, hs_sem):
                k4 = [P, KT, NB, NS]
                ch.link(dve.scalar_tensor_tensor(s_, mod[:, m_scale:m_scale + KT, :], 1.0,
                                                 vec[:, v_g:v_g + KT].unsqueeze(2).to_broadcast([P, KT, CB]), ALU.add, ALU.mult))
                ch.link(dve.tensor_tensor(v_.rearrange("p (k n) -> p k n", n=SAMP), X[:, :, SEQ:T],
                                          rstd[:, SEQ:T].unsqueeze(1).to_broadcast([P, KT, SAMP]), ALU.mult))
                t4 = t_.rearrange("p (k b t) -> p k b t", b=NB, t=NS)
                ch.link(dve.tensor_tensor(t4, v_.rearrange("p (k b t) -> p k b t", b=NB, t=NS),
                                          s_[:, :, 0:NB].unsqueeze(3).to_broadcast(k4), ALU.mult))
                dve.tensor_tensor(t4, t4, mod[:, m_shift:m_shift + KT, 0:NB].unsqueeze(3).to_broadcast(k4), ALU.add) \
                   .then_inc(hs_sem, 1)

            def modulated(s_, t_, halves, rstd, m_shift, names4):
                hp_ready, hi_sem, hi_s, ready = (sem(n) for n in names4)

                def scaled(k):
                    if k >= 2:
                        dve.wait_ge(ready, k - 1)
                    dve.scalar_tensor_tensor(halves[k % 2], X[:, k, 0:SEQ], s_[:, k, 8:9], rstd[:, 0:SEQ],
                                             ALU.mult, ALU.mult).then_inc(hp_ready, 1)
                scaled(0)
                for k in range(KT):
                    if k + 1 < KT:
                        scaled(k + 1)
                    if k == 0:
                        dve.wait_ge(hi_s, 1)
                        dve.tensor_tensor(act_lo[:, :, SEQ:T], t_.rearrange("p (k n) -> p k n", n=SAMP),
                                          act_hi[:, :, SEQ:T].bitcast(F32), ALU.subtract)
                    dve.wait_ge(hi_sem, k + 1)
                    dve.scalar_tensor_tensor(act_lo[:, k, 0:SEQ], halves[k % 2], mod[:, m_shift + k, 8:9],
                                             act_hi[:, k, 0:SEQ].bitcast(F32), ALU.add, ALU.subtract).then_inc(ready, 1)

            dve.wait_ge(sem("rs_ready"), 1)
            dve.wait_ge(sem("bank4_taken"), 8)
            ch.enter(0, 3)
            modulate(s1, mod_t, mod_u, rs, 16, 0, V_G1, sem("hs_ready"))
            ch.leave()
            ch.advance(3)
            modulated(s1, mod_t, hp, rs, 0, ("hp_ready", "x1_hi", "x1_hi_s", "x1_ready"))

            def softplus(i):
                dve.wait_ge(sem("scores_mm"), i)
                hb = bias_h[:, bass.ds(i - 1, 1)]
                for b, j0, n in ((5, 0, 512), (6, 512, 384), (7, 896, 384)):
                    ins = dve.tensor_scalar(zf[:, j0:j0 + n], ps[:, b, 0:n], SCALE, hb, ALU.mult, ALU.add)
                ins.then_inc(sem("z_taken"), 1)
                dve.wait_ge(sem("z_taken"), i)
                dve.wait_ge(sem("lz_ready"), i)
                dve.scalar_tensor_tensor(sp_[:], zf[:], 0.0, wt[:], ALU.max, ALU.add).then_inc(sem("sp_whole"), 1)
                dve.wait_ge(sem("sp_whole"), 2 * i - 1)
                dve.tensor_tensor(zf[:], zf[:], sp_[:], ALU.subtract).then_inc(sem("sp_whole"), 1)
                dve.wait_ge(sem("sp_whole"), 2 * i)
                for j in J0:
                    ins = dve.tensor_tensor(sp_[:, j:j + P], sp_[:, j:j + P], before[:], ALU.mult)
                ins.then_inc(sem("sp_ready"), 1)

            def log_weights(i):
                dve.wait_ge(sem("sums_mm"), i)
                dve.wait_ge(sem("sp_ready"), i)
                for b, j0, n in ((5, 0, 512), (6, 512, 384), (7, 896, 384)):
                    ins = dve.tensor_tensor(zf[:, j0:j0 + n], ps[:, b, 0:n], zf[:, j0:j0 + n], ALU.add)
                ins.then_inc(sem("arg_ready"), 1)
                dve.wait_ge(sem("w_exp"), i)
                for j in J0:
                    ins = dve.tensor_tensor(wt[:, j:j + P], wt[:, j:j + P], before[:], ALU.mult)
                ins.then_inc(sem("w_ready"), 1)

            def take_k(i):
                dve.wait_ge(sem("kv_turned"), i)
                if not isinstance(i, int) or i > 1:
                    dve.wait_ge(sem("k_stored"), 16 * i - 16)
                dve.tensor_copy(kn[:], ps[:, 3, :].rearrange("p (t d) -> p t d", d=P)).then_inc(sem("kn_taken"), 1)

            def take_sample(i):
                if not isinstance(i, int) or i > 1:
                    dve.wait_ge(sem("ks_stored"), 16 * i - 16)
                b4 = ps[0:SAMP, 4, :]
                h = bass.ds(i - 1, 1)
                dve.tensor_copy(vs[:, h, :].rearrange("p a d -> p (a d)"), b4[:, 128:256])
                dve.tensor_copy(ksn[:], b4[:, 256:384])
                dve.tensor_copy(zs[0:SAMP, h, :].rearrange("p a d -> p (a d)"), b4[:, 384:448]).then_inc(sem("bank4_taken"), 1)

            def qkv(i):
                u, prev = turn(B_QKV, i, 12), not starts(i)
                for k in range(4, 8):
                    lo(u, k)
                if prev:
                    softplus(i)
                for k in range(8, 12):
                    lo(u, k)
                if prev:
                    log_weights(i)
                lo(u, 12)
                if prev:
                    take_k(i)
                for k in range(13, 16):
                    lo(u, k)
                take_mod(u, 12, 3, 32 + 3 * i, 8 + i, done=not prev)
                if prev:
                    take_sample(i)
                dve.wait_ge(sem("rq_ready"), i + 1)
                dve.scalar_tensor_tensor(qf[:], qraw[:], vec[:, V_GQ:V_GQ + 1], sqq[:], ALU.mult, ALU.mult) \
                   .then_inc(sem("qf_ready"), 1)
                dve.wait_ge(sem("qf_ready"), i + 1)
                dve.tensor_copy(qs[:, bass.ds(i, 1), :].rearrange("p a n -> p (a n)"), qf[:, SEQ:T])
                dve.wait_ge(sem("rk_ready"), i + 1)
                dve.scalar_tensor_tensor(kf[:], kraw[:], vec[:, V_GK:V_GK + 1], sqk[:], ALU.mult, ALU.mult) \
                   .then_inc(sem("qk_ready"), 1)
            turns(dve, NH, qkv, 2)
            softplus(NH)
            log_weights(NH)
            take_k(NH)
            take_sample(NH)

            dve.wait_ge(sem("x_saved"), 16)
            dve.wait_ge(sem("zs_zeroed"), 1)
            dve.wait_ge(sem("o_taken"), NH)
            dve.wait_ge(sem("v_stored"), 16 * NH)
            dve.wait_ge(sem("k_stored"), 16 * NH)
            dve.wait_ge(sem("ks_stored"), 16 * NH)
            dve.wait_ge(sem("bank4_taken"), 17)
            z3, zf_ = zs[0:SAMP], zs[0:SAMP].rearrange("p h q -> p (h q)")
            same3 = same[:].unsqueeze(1).to_broadcast([SAMP, NH, SAMP])
            ch.enter(0, 5)
            dve.scalar_tensor_tensor(z3, z3, SCALE, bias_h[0:SAMP, :].unsqueeze(2).to_broadcast([SAMP, NH, SAMP]),
                                     ALU.mult, ALU.add).then_inc(sem("self_z"), 1)
            dve.wait_ge(sem("self_z"), 1)
            dve.wait_ge(sem("self_l"), 1)
            ch.link(dve.scalar_tensor_tensor(wself[:], zf_, 0.0, wself[:], ALU.max, ALU.add))
            ch.link(dve.tensor_tensor(spc[0:SAMP, :], zf_, wself[:], ALU.subtract))
            w3 = wself[:].rearrange("p (h q) -> p h q", q=SAMP)
            dve.tensor_tensor(z3, w3, same3, ALU.mult).then_inc(sem("self_sp_ready"), 1)
            dve.wait_ge(sem("self_mm"), 1)
            dve.wait_ge(sem("self_sp_ready"), 1)
            dve.tensor_tensor(spc[0:SAMP, :], ps[0:SAMP, 7, :], spc[0:SAMP, :], ALU.add).then_inc(sem("self_arg"), 1)
            dve.wait_ge(sem("self_w"), 1)
            dve.tensor_tensor(w3, w3, same3, ALU.mult).then_inc(sem("self_done"), 1)
            dve.wait_ge(sem("c8_parts"), 1)
            ch.link(dve.tensor_tensor(c8[:, 0, :], c8[:, 0, :], c8[:, 1, :], ALU.add))
            ch.link(dve.tensor_scalar(c8[:, 1, :], c8[:, 0, :], LRU_C, None, ALU.mult))
            ch.link(dve.tensor_scalar(c8[:, 0, :], c8[:, 0, :], -LRU_C, None, ALU.mult))
            dve.memset(xlp[:, 0:3], 0.0)
            for s in range(PAGES):
                ins = dve.tensor_copy(bias_z[:, s * 64:(s + 1) * 64].rearrange("p (h q) -> p h q", q=NS),
                                      bias_h[:].unsqueeze(2).to_broadcast([P, NH, NS]))
            ins.then_inc(sem("c8_ready"), 1)
            dve.wait_ge(sem("c8_ready"), 1)
            ch.leave()
            ch.advance(5)

            ends = bass.ds(SEQ, SAMP)

            def recurrence(i):
                n = i - 1
                xd = xlp[:, 3:3 + T]
                dve.wait_ge(sem("a_ready"), 2 * i)
                ch.link(dve.tensor_tensor(La[:], Lc[:], Lc[:], ALU.mult))
                dve.scalar_tensor_tensor(xd, La[:], 1.0, xd, ALU.add, ALU.mult).then_inc(sem("m2_ready"), 1)
                dve.wait_ge(sem("i_taken"), i)
                ch.link(dve.tensor_tensor(Lb[:], Lb[:], xc[:], ALU.mult))
                dve.wait_ge(sem("m_ready"), i)
                ch.link(dve.memset(xd[:, 0:1], 1.0))
                ch.link(dve.tensor_tensor(Lb[:], Lb[:], xd, ALU.mult))
                a_s = Lc[:, SEQ:T].rearrange("p (b t) -> p b t", t=NS)[:, :, 0:1]
                b_s = Lb[:, SEQ:T].rearrange("p (b t) -> p b t", t=NS)[:, :, 0:1]
                h0 = lst[:, 192:256].rearrange("p (b n) -> p b n", n=NL)[:, :, bass.ds(n, 1)]
                t8 = La[:, 0:NB].unsqueeze(2)
                ch.link(dve.tensor_tensor(t8, a_s, h0, ALU.mult))
                ch.link(dve.tensor_tensor(b_s, b_s, t8, ALU.add))
                ch.link(dve.memset(a_s, 0.0))
                ch.step(dve.tensor_tensor_scan(xc[:, 0:SEQ], Lc[:, 0:SEQ], Lb[:, 0:SEQ], 0.0, ALU.mult, ALU.add))
                ch.link(dve.tensor_tensor_scan(xc[:, SEQ:T], Lc[:, SEQ:T], Lb[:, SEQ:T], 0.0, ALU.mult, ALU.add))
                dve.tensor_copy(lnew[:, bass.ds(n + 216, 1)], xc[:, SEQ - 1:SEQ])
                dve.tensor_copy(lnew[:, 224:288].rearrange("p (b n) -> p b n", n=NL)[:, :, bass.ds(n, 1)],
                                xc[:, SEQ:T].rearrange("p (b t) -> p b t", t=NS)[:, :, NS - 1:NS])
                dve.tensor_tensor(X[:, bass.ds(n + NH, 1), :].rearrange("p a n -> p (a n)"), xc[:], gg[:], ALU.mult) \
                   .then_inc(sem("lru_done"), 1)

            def take_keys(i, s):
                dve.wait_ge(sem("kb_turned"), 8 * i + (s + 1))
                wait(dve, sem("kb_used"), 8 * i + s)
                dve.tensor_copy(kt_[1][:], ps[:, 6, :].rearrange("p (h k) -> p h k", k=P)).then_inc(sem("kb_taken"), 1)

            RS, LS = 9, 17

            def lru(i):
                u = turn(B_LRU, i, 12)
                if isinstance(i, int):
                    ch.enter(0, LS)
                else:
                    ch.enter((LS + RS) * i - RS, LS + RS)
                    recurrence(i)
                lo(u, 4)
                for s in range(4):
                    take_keys(i, s)
                lo(u, 5)
                dve.wait_ge(sem("xl_out"), 3 * i + 3)
                ch.link(dve.tensor_copy(xlp_s[:, :, 0:3], lst[:, 0:192].rearrange("p (b w n) -> p b w n", w=3, n=NL)
                                        [:, :, :, bass.ds(i, 1)].rearrange("p b w n -> p b (w n)")))
                xc_s = xc[:, SEQ:T].rearrange("p (b t) -> p b t", t=NS)
                for w in (3, 2, 1, 0):
                    col = vec[:, bass.ds(V_LCW + w * NL + i, 1)]
                    if w == 3:
                        bcol = vec[:, bass.ds(V_LCB + i, 1)]
                        ch.step(dve.tensor_scalar(xc[:, 0:SEQ], xlp[:, w:w + SEQ], col, bcol, ALU.mult, ALU.add))
                        ch.link(dve.tensor_scalar(xc_s, xlp_s[:, :, w:w + NS], col, bcol, ALU.mult, ALU.add))
                    else:
                        ch.step(dve.scalar_tensor_tensor(xc[:, 0:SEQ], xlp[:, w:w + SEQ], col, xc[:, 0:SEQ], ALU.mult, ALU.add))
                        ins = dve.scalar_tensor_tensor(xc_s, xlp_s[:, :, w:w + NS], col, xc_s, ALU.mult, ALU.add)
                        if w:
                            ch.link(ins)
                        else:
                            ins.then_inc(sem("xc_ready"), 1)
                for k in range(6, 10):
                    lo(u, k)
                for s in range(4, 8):
                    take_keys(i, s)
                dve.wait_ge(sem("ka_used"), 8 * i + 8)
                dve.wait_ge(sem("kb_used"), 8 * i + 8)
                dve.scalar_tensor_tensor(zc[:], ps[:, 7, :], SCALE, bias_z[:], ALU.mult, ALU.add).then_inc(sem("zc_taken"), 1)
                dve.wait_ge(sem("zc_taken"), i + 1)
                dve.wait_ge(sem("lc_ready"), i + 1)
                ch.link(dve.scalar_tensor_tensor(spc[:], zc[:], 0.0, spc[:], ALU.max, ALU.add))
                ch.step(dve.tensor_tensor(zc[:], zc[:], spc[:], ALU.subtract))
                wait(dve, sem("o2_mm"), i)
                ch.link(dve.tensor_copy(suf[:, 448:512].rearrange("p (h q) -> p h q", q=NS), zs[:, :, bass.ds(NS * i, NS)]))
                for s in range(6, -1, -1):
                    ins = dve.tensor_tensor(suf[:, s * 64:(s + 1) * 64], suf[:, (s + 1) * 64:(s + 2) * 64],
                                            spc[:, (s + 1) * 64:(s + 2) * 64], ALU.add)
                    if s:
                        ch.link(ins)
                    else:
                        ins.then_inc(sem("spc_ready"), 1)
                lo(u, 10)
                dve.wait_ge(sem("sums2_mm"), i + 1)
                dve.tensor_tensor(zc[:], ps[:, 7, :], zc[:], ALU.add).then_inc(sem("argc_ready"), 1)
                for k in range(11, 16):
                    lo(u, k)
                take_mod(u, 12, 4, 56 + 4 * i, 16 + i)
                ch.leave()
            turns(dve, NL, lru)
            ch.advance((LS + RS) * NL - RS)
            ch.enter(0, RS)
            recurrence(NL)
            ch.leave()
            ch.advance(RS)

            dve.wait_ge(sem("lru_done"), NL)
            for k in range(KT):
                dve.wait_ge(sem("mix_hi"), k + 1)
                dve.tensor_tensor(act_lo[:, k, :], X[:, k, :], act_hi[:, k, :].bitcast(F32), ALU.subtract) \
                   .then_inc(sem("mix_ready"), 1)

            def gated(m, bank, gate, gate_s, base, base_s, t, done):
                tile_ = X[:, bass.ds(m, 1), :].rearrange("p a n -> p (a n)")
                dve.tensor_tensor(t, ps[:, bank + 1, SEQ - HALF:HALF].rearrange("p (b t) -> p b t", t=NS),
                                  gate_s.to_broadcast([P, NB, NS]), ALU.mult).then_inc(sem("gated_part"), 1)
                dve.scalar_tensor_tensor(tile_[:, 0:HALF], ps[:, bank, 0:HALF], gate, base[:, 0:HALF], ALU.mult, ALU.add)
                dve.scalar_tensor_tensor(tile_[:, HALF:SEQ], ps[:, bank + 1, 0:SEQ - HALF], gate, base[:, HALF:SEQ],
                                         ALU.mult, ALU.add)
                return dve.tensor_tensor, (tile_[:, SEQ:T].rearrange("p (b t) -> p b t", t=NS), t, base_s, ALU.add)

            def out(i):
                u = turn(B_OUT, i, 12)
                for j in range(4):
                    k, m = (0, 2, 6, 8)[j], 4 * i + j
                    lo(u, k + 4)
                    lo(u, k + 5)
                    if j % 2:
                        lo(u, k + 6)
                        lo(u, k + 7)
                    dve.wait_ge(blk_used, u[0] + (k + 2))
                    dve.wait_ge(sem(f"xres_loaded{j % 2}"), 32 * i + 16 * (j // 2 + 1))
                    if isinstance(i, int) and j == 0:
                        dve.wait_ge(sem("mix_ready"), KT)
                    base = xres[:, j % 2, :]
                    gt = mod[:, bass.ds(4 * i + (32 + j), 1), :].rearrange("p a c -> p (a c)")
                    f, a = gated(m, 2 * (j % 2), gt[:, 8:9], gt[:, 0:NB].unsqueeze(2), base,
                                 base[:, SEQ:T].rearrange("p (b t) -> p b t", t=NS),
                                 t64[:, j % 2, :].rearrange("p (b t) -> p b t", t=NS), None)
                    dve.wait_ge(sem("gated_part"), 4 * i + (j + 1))
                    f(*a).then_inc(sem("x2_ready"), 1)
                take_mod(u, 12, 2, 88 + 2 * i, 24 + i)
            turns(dve, 4, out)

            dve.wait_ge(sem("rs2_ready"), 1)
            dve.wait_ge(sem("x2_ready"), KT)
            dve.wait_ge(sem("bank4_taken"), 29)
            dve.wait_ge(blk_used, B_FFN)
            ch.enter(0, 3)
            modulate(s2[:], mt2[:, 0, :], mt2[:, 1, :], rs2, 64, 48, V_G2, sem("hs2_ready"))
            ch.leave()
            ch.advance(3)
            modulated(s2, mt2[:, 0, :], [hp2[:, 0, :], hp2[:, 1, :]], rs2, 48, ("hp2_ready", "x3_hi", "x3_hi_s", "x3_ready"))
            dve.wait_ge(sem("lnew_turned"), 1)
            dve.tensor_copy(crl[:, 0:256], ps[:, 2, 0:256]).then_inc(sem("lnew_taken"), 1)
            dve.tensor_copy(crl[0:32, 256:384], ps[0:32, 2, 256:384]).then_inc(sem("lnew_taken"), 1)

            dve.wait_ge(sem("x3_ready"), KT)
            for w in range(2):
                dve.memset(up[w][:, 0:2], 0.0)
            dve.wait_ge(sem("cv_taken"), 3)

            def convolve(which, nt, out_sem, done):
                dve.wait_ge(out_sem, 3 * nt + 3)
                m = nt + NFF * which
                ch.link(dve.tensor_copy(up_s[which][:, :, 0:2], cv[:, 2:18, bass.ds(m, 1)].rearrange("p (b w) c -> p b (w c)", w=2)))
                uc_s = uc[which][:, SEQ:T].rearrange("p (b t) -> p b t", t=NS)
                for w in (2, 1, 0):
                    col = vec[:, bass.ds(m + (V_FCW + w * NM), 1)]
                    if w == 2:
                        bcol = vec[:, bass.ds(m + V_FCB, 1)]
                        ch.step(dve.tensor_scalar(uc[which][:, 0:SEQ], up[which][:, w:w + SEQ], col, bcol, ALU.mult, ALU.add))
                        ch.link(dve.tensor_scalar(uc_s, up_s[which][:, :, w:w + NS], col, bcol, ALU.mult, ALU.add))
                    else:
                        ch.step(dve.scalar_tensor_tensor(uc[which][:, 0:SEQ], up[which][:, w:w + SEQ], col,
                                                         uc[which][:, 0:SEQ], ALU.mult, ALU.add))
                        ins = dve.scalar_tensor_tensor(uc_s, up_s[which][:, :, w:w + NS], col, uc_s, ALU.mult, ALU.add)
                        if w:
                            ch.link(ins)
                        else:
                            ins.then_inc(done, 1)

            def up_tile(g, j):
                u, nt = ffn_up(g, j), G * g + j
                ch.enter(12 * nt, 12)
                lo(u, 4)
                lo(u, 5)
                convolve(0, nt, sem("gate_out"), sem("gate_conv"))
                lo(u, 6)
                lo(u, 7)
                convolve(1, nt, sem("value_out"), sem("value_conv"))
                dve.wait_ge(sem("value_conv"), nt + 1)
                dve.wait_ge(sem("gelu_done"), nt + 1)
                dve.tensor_tensor(gp[:], uc[0][:], uc[1][:], ALU.mult).then_inc(sem("gp_ready"), 1)
                dve.wait_ge(sem("gp_ready"), nt + 1)
                dve.wait_ge(sem("g_hi_ready"), nt + 1)
                h = bass.ds(j, 1)
                dve.tensor_tensor(g_lo[:, h, :].rearrange("p a n -> p (a n)"), gp[:],
                                  g_hi[:, h, :].rearrange("p a n -> p (a n)").bitcast(F32), ALU.subtract).then_inc(sem("g_ready"), 1)
                ch.leave()

            def down(g, last):
                def four(m, end=False):
                    u = ffn_down(g, m)
                    for c in range(4):
                        if not end:
                            lo(u, c + 4)
                        mm = 4 * m + c
                        tiles = KT * g + mm
                        dve.wait_ge(blk_used, u[0] + (c + 1))
                        wait(dve, sem("y_taken"), tiles)
                        tile_ = X[:, bass.ds(mm, 1), :].rearrange("p a n -> p (a n)")
                        gt = mod[:, bass.ds(mm + 80, 1), :].rearrange("p a c -> p (a c)")
                        ts_ = tile_[:, SEQ:T].rearrange("p (b t) -> p b t", t=NS)
                        f, a = gated(mm, 2 * (c % 2), gt[:, 8:9], gt[:, 0:NB].unsqueeze(2), tile_, ts_,
                                     t64b[:, c % 2, :].rearrange("p (b t) -> p b t", t=NS), None)
                        dve.wait_ge(sem("gated_part"), tiles + (KT + 1))
                        f(*a).then_inc(sem("y_taken"), 1)
                four(0)
                with dve.Fori(1, 3) as m:
                    four(m)
                four(3, last)

            def group(g, last=False):
                if isinstance(g, int) and g == 0:
                    up_tile(0, 0)
                    with dve.Fori(1, G) as j:
                        up_tile(0, j)
                else:
                    with dve.Fori(0, G) as j:
                        up_tile(g, j)
                down(g, last)
            group(0)
            with dve.Fori(1, NG - 1) as g:
                group(g)
            group(NG - 1, True)

            for n in range(1, 24, 2):
                dve.wait_ge(sem("y_turned"), n + 1)
                t, q = n // 4, n % 4
                w = P if t != 4 else SAMP
                if t < 5:
                    if t >= 2 and q == 1:
                        dve.wait_ge(sem(f"y_stored{t % 2}"), 16 * (t // 2))
                    dve.tensor_copy(yr[0:w, t % 2, q * 512:(q + 1) * 512], ps[0:w, n % 8, :]).then_inc(sem("y_odd"), 1)
                elif q == 1:
                    dve.tensor_copy(crt[:, 4:8, :], ps[:, n % 8, :].rearrange("p (a b) -> p a b", b=P)).then_inc(sem("y_odd"), 1)
                else:
                    dve.tensor_copy(crt[:, 12, :], ps[:, n % 8, 0:P])
                    dve.tensor_copy(crt[0:64, 13, :], ps[0:64, n % 8, P:2 * P]).then_inc(sem("y_odd"), 1)

        @block.gpsimd
        def _(pool):
            def hold(name, value):
                wait(pool, sem(name), value)
                if not isinstance(value, int):
                    pool.sem_inc(sem("pool_waits"), 1)

            pool.memset(X[0:CB].rearrange("p k n -> p (k n)")[:, 0:D], 0.0).then_inc(sem("zeroed"), 1)
            pool.memset(vr[:, 1, :], 0.0).then_inc(sem("zeroed"), 1)
            pool.memset(eps[:], EPS)
            pool.memset(neg_ones[:], -1.0)
            pool.memset(ident[:], 0.0)
            pool.memset(neg_later[:], -1.0)
            pool.memset(before[:], 1.0)
            pool.memset(same[:], 1.0).then_inc(sem("filled"), 1)
            pool.wait_ge(sem("filled"), 1)
            pool.affine_select(out=ident[:], in_=ident[:], compare_op=ALU.not_equal, fill=1.0, base=0,
                               pattern=[[-1, P]], channel_multiplier=1)
            pool.affine_select(out=neg_later[:], in_=neg_later[:], compare_op=ALU.is_gt, fill=0.0, base=0,
                               pattern=[[-1, P]], channel_multiplier=1)
            pool.affine_select(out=before[:], in_=before[:], compare_op=ALU.is_gt, fill=0.0, base=0,
                               pattern=[[1, P]], channel_multiplier=-1)
            same3 = same[:].rearrange("p (b t) -> p b t", t=NS)
            pool.affine_select(out=same3, in_=same3, compare_op=ALU.is_gt, fill=0.0, base=0,
                               pattern=[[NS, NB], [1, NS]], channel_multiplier=-1).then_inc(sem("filled"), 1)
            pool.wait_ge(sem("filled"), 2)
            pool.affine_select(out=same3, in_=same3, compare_op=ALU.is_ge, fill=0.0, base=0,
                               pattern=[[-NS, NB], [0, NS]], channel_multiplier=1).then_inc(sem("consts"), 1)
            pool.dma_start(bias_h[:], b_sb.to_broadcast([P, NH])).then_inc(sem("bias_loaded"), 16)
            pool.wait_ge(sem("bias_loaded"), 16)
            pool.wait_ge(sem("x1_ready"), KT)
            pool.memset(zs[SAMP:P], 0.0).then_inc(sem("zs_zeroed"), 1)

            kpo = k_prompt[0, 0].rearrange("t p h d -> p t h d")
            vpo = v_prompt[0, 0].rearrange("t p h d -> p t h d")
            kso = k_sample[0].rearrange("b t h d -> (b t) h d")
            vso = v_sample[0].rearrange("b t h d -> (b t) h d")

            def store(i):
                h = bass.ds(i - 1, 1)
                hold("vn_taken", i)
                pool.dma_start(vpo[:, :, h, :].rearrange("p t h d -> p t (h d)"), vn[:]).then_inc(sem("v_stored"), 16)
                hold("kn_taken", i)
                pool.dma_start(kpo[:, :, h, :].rearrange("p t h d -> p t (h d)"), kn[:]).then_inc(sem("k_stored"), 16)
                hold("bank4_taken", i + 9)
                pool.dma_start(kso[:, h, :].rearrange("p h d -> p (h d)"), ksn[:]).then_inc(sem("ks_stored"), 16)
            with pool.Fori(1, NH + 1) as i:
                store(i)
            pool.dma_start(vso.rearrange("p h d -> p (h d)"), vs[:].rearrange("p h d -> p (h d)")).then_inc(sem("vs_stored"), 16)

            pool.wait_ge(sem("self_z"), 1)
            pool.dma_start(pt[:], page_table.rearrange("b p -> (b p)").unsqueeze(0)).then_inc(sem("pt_loaded"), 16)
            pool.wait_ge(sem("pt_loaded"), 16)
            ck = cache_k[0].rearrange("n p h d -> n p (h d)")
            cvv = cache_v[0].rearrange("n p h d -> n p (h d)")
            npool = cache_k.shape[1]

            def page(i, s):
                return pool.value_load(pt[0:1, bass.ds(8 * i + s, 1)], min_val=0, max_val=npool - 1)

            def load(i, s, dst, src, name, free):
                v = page(i, s)
                hold(free, 8 * i + (s - 1))
                pool.dma_start(dst[s % 2][:].rearrange("p h d -> p (h d)"),
                               src[bass.ds(v, 1)].rearrange("n p c -> p (n c)")).then_inc(sem(f"{name}{s % 2}"), 16)

            def lru(i):
                hold("i_mm", i)
                pool.dma_start(wg[:, 0, :], w_lru_a[0, bass.ds(i, 1)].rearrange("a c d -> c (a d)")).then_inc(sem("gates_loaded"), 16)
                pool.dma_start(wg[:, 1, :], w_lru_x[0, bass.ds(i, 1)].rearrange("a c d -> c (a d)")).then_inc(sem("gates_loaded"), 16)
                for s in range(6):
                    load(i, s, kpg, ck, "k_loaded", "kb_turned")
                for s in range(2):
                    load(i, s, vpg, cvv, "v_loaded", "v_used")
                pool.wait_ge(sem("xl_out"), 3 * i + 3)
                pool.tensor_copy(lnew[:, 0:24].rearrange("p (r n) -> p r n", n=NL)[:, :, bass.ds(i, 1)],
                                 xlp[:, SEQ:SEQ + 3].unsqueeze(2)).then_inc(sem("lnew_saved"), 1)
                pool.tensor_copy(lnew[:, 24:216].rearrange("p (b w n) -> p b w n", w=3, n=NL)[:, :, :, bass.ds(i, 1)]
                                 .rearrange("p b w n -> p b (w n)"), xlp_s[:, :, 8:11]).then_inc(sem("lnew_saved"), 1)
                for s in range(6, 8):
                    load(i, s, kpg, ck, "k_loaded", "kb_turned")
                for s in range(2, 8):
                    load(i, s, vpg, cvv, "v_loaded", "v_used")
            turns(pool, NL, lru)

            pool.wait_ge(sem("lru_done"), NL)
            pool.wait_ge(sem("o2_taken"), NL)
            pool.wait_ge(sem("vs_stored"), 16)
            pool.dma_start(str_[:], state_ffn_conv.rearrange("a b w (r c) -> (a b w r) c", c=P)
                           .rearrange("(j p) c -> p j c", p=P)).then_inc(sem("ffn_state_loaded"), 16)
            xs_v = x_save.rearrange("p (k n) -> p k n", n=T)
            pool.wait_ge(sem("x_saved"), 16)

            def residual(i):
                for j in range(4):
                    hold("x2_ready", 4 * i + (j - 1))
                    pool.dma_start(xres[:, j % 2, :], xs_v[:, bass.ds(4 * i + j, 1), :].rearrange("p a n -> p (a n)")) \
                        .then_inc(sem(f"xres_loaded{j % 2}"), 16)
            turns(pool, 4, residual)

            stored = sem("states_stored")
            pool.wait_ge(sem("lnew_taken"), 2)
            cl = lru_conv_prompt.rearrange("a b w (r c) -> (a b w r) c", c=P)
            cls = lru_conv_sample.rearrange("a b w (r c) -> (a b w r) c", c=P)
            hs = lru_h_sample.rearrange("a b (r c) -> (a b r) c", c=P)
            pool.dma_start(cl, crl[0:24, 0:P]).then_inc(stored, 16)
            pool.dma_start(cls[0:104], crl[24:128, 0:P]).then_inc(stored, 16)
            pool.dma_start(cls[104:192], crl[0:88, P:2 * P]).then_inc(stored, 16)
            pool.dma_start(lru_h_prompt.rearrange("a b (r c) -> (a b r) c", c=P), crl[88:96, P:2 * P]).then_inc(stored, 16)
            pool.dma_start(hs[0:32], crl[96:128, P:2 * P]).then_inc(stored, 16)
            pool.dma_start(hs[32:64], crl[0:32, 2 * P:3 * P]).then_inc(stored, 16)
            pool.wait_ge(stored, 96)

            def save(which, nt, conv_sem, out_sem):
                pool.wait_ge(conv_sem, nt + 1)
                m = bass.ds(nt + NFF * which, 1)
                pool.tensor_copy(cv[:, 0:2, m], up[which][:, SEQ:SEQ + 2].unsqueeze(2)).then_inc(sem("cv_saved"), 1)
                pool.tensor_copy(cv[:, 2:18, m].rearrange("p (b w) c -> p b (w c)", w=2), up_s[which][:, :, 8:10]).then_inc(sem("cv_saved"), 1)

            def states(nt):
                save(0, nt, sem("gate_conv"), None)
                save(1, nt, sem("value_conv"), None)
            turns(pool, NFF, states)

            pool.wait_ge(sem("y_even"), 12)
            pool.wait_ge(sem("y_odd"), 12)
            fp = ffn_conv_prompt.rearrange("a b w (r c) -> (a b w r) c", c=P)
            fs = ffn_conv_sample.rearrange("a b w (r c) -> (a b w r) c", c=P)
            pool.dma_start(fp[0:128], crt[:, 0, :]).then_inc(stored, 16)
            pool.dma_start(fp[128:192], crt[0:64, 1, :]).then_inc(stored, 16)
            pool.dma_start(fs[0:64], crt[64:128, 1, :]).then_inc(stored, 16)
            pool.dma_start(fs[64:64 + 11 * P].rearrange("(j p) c -> p j c", p=P), crt[:, 2:13, :]).then_inc(stored, 16)
            pool.dma_start(fs[64 + 11 * P:1536], crt[0:64, 13, :]).then_inc(stored, 16)
            pool.wait_ge(stored, 176)


_INS = ['x_prompt', 'x_sample', 'c_prompt', 'c_sample', 'cache_k', 'cache_v', 'page_table',
        'state_lru_conv', 'state_lru_h', 'state_ffn_conv',
        'w_ada', 'b_ada', 'g_norm1', 'w_in', 'g_q', 'g_k', 'b_sb', 'w_lru_conv', 'b_lru_conv',
        'w_lru_a', 'b_lru_a', 'w_lru_x', 'b_lru_x', 'lru_lambda', 'w_out',
        'g_norm2', 'w_up', 'w_ffn_conv', 'b_ffn_conv', 'w_down']
_OUTS = [(1, 512, 2048), (8, 8, 2048), (1, 1, 4, 128, 8, 128), (1, 1, 4, 128, 8, 128), (1, 8, 8, 8, 128),
         (1, 8, 8, 8, 128), (1, 1, 3, 1024), (1, 8, 3, 1024), (1, 1, 1024), (1, 8, 1024),
         (1, 1, 2, 12288), (1, 8, 2, 12288)]


def kernel(**inputs):
    import numpy as _np
    import concourse.bacc as _bacc
    from concourse import mybir as _mybir
    from concourse.bass_utils import run_bass_kernel_spmd as _run

    nc = _bacc.Bacc("TRN2", target_bir_lowering=False, num_devices=1, dynamic_dma_scratch_size=2560)
    arrays, args = {}, []
    for name in _INS:
        a = _np.ascontiguousarray(inputs[name])
        arrays[f"in_{name}_dram"] = a
        args.append(nc.dram_tensor(f"in_{name}_dram", a.shape, _mybir.dt.from_np(a.dtype), kind="ExternalInput").ap())
    for i, shape in enumerate(_OUTS):
        args.append(nc.dram_tensor(f"out_{i}_dram", shape, F32, kind="ExternalOutput").ap())
    build(nc, *args)
    r = _run(nc, [arrays], core_ids=[0])
    return tuple(r.results[0][f"out_{i}_dram"] for i in range(len(_OUTS)))
```

```python
from contextlib import ExitStack

import concourse.bass as bass
from concourse import mybir

F32 = mybir.dt.float32
F32R = mybir.dt.float32r
I32 = mybir.dt.int32
ALU = mybir.AluOpType
ACT = mybir.ActivationFunctionType

P = 128
D = 2048
KT = D // P
SEQ = 512
NB = 8
NS = 8
SAMP = NB * NS
T = SEQ + SAMP
HALF = T // 2
NH = 8
NL = 8
PAGES = 8
KB = 8
SLOTS = 4
NFF = 48
G = 6
NG = NFF // G
NM = 96
CB = 10
EPS = 1e-6
SCALE = float(P) ** -0.5
LRU_C = 8.0

V_BADA, V_G1, V_G2 = 0, 96, 112
V_LCW, V_LCB, V_BA, V_BX, V_LAM, V_GQ, V_GK = 128, 160, 168, 176, 184, 192, 193
V_FCW, V_FCB = 256, 544
B_ADA, B_QKV, B_LRU, B_OUT, B_FFN = 0, 64, 128, 256, 304
J0 = (0, 512, 896, 1152)
QW = (512, 384, 256, 128)
ZB = ((5, 0), (6, 0), (7, 0), (7, 256))


def wait(eng, sem, value):
    if not isinstance(value, int) or value > 0:
        eng.wait_ge(sem, value)


def turns(eng, n, body, straight=1):
    for i in range(straight):
        body(i)
    with eng.Fori(straight, n) as i:
        body(i)


def starts(i):
    return isinstance(i, int) and i == 0


def turn(base, i, per):
    return base + per * i, base // SLOTS + (per // SLOTS) * i


def ffn_up(g, j):
    return B_FFN + 40 * g + 4 * j, B_FFN // SLOTS + 10 * g + j


def ffn_down(g, m):
    return B_FFN + 40 * g + 24 + 4 * m, B_FFN // SLOTS + 10 * g + 6 + m


class Chain:

    def __init__(self, eng, sem):
        self.eng, self.sem, self.start, self.base, self.n = eng, sem, 0, 0, 0

    def enter(self, offset, per):
        self.base, self.per, self.n = offset + self.start, per, 0

    def leave(self):
        assert self.n == self.per, f"{self.n} steps, not {self.per}"

    def advance(self, total):
        self.start += total

    def step(self, ins):
        ins.then_inc(self.sem, 1)
        self.n += 1

    def settle(self):
        self.eng.wait_ge(self.sem, self.base + self.n)

    def link(self, ins):
        self.step(ins)
        self.settle()


def build(nc, x_prompt, x_sample, c_prompt, c_sample, cache_k, cache_v, page_table,
          state_lru_conv, state_lru_h, state_ffn_conv,
          w_ada, b_ada, g_norm1, w_in, g_q, g_k, b_sb, w_lru_conv, b_lru_conv,
          w_lru_a, b_lru_a, w_lru_x, b_lru_x, lru_lambda, w_out,
          g_norm2, w_up, w_ffn_conv, b_ffn_conv, w_down,
          y_prompt, y_sample, k_prompt, v_prompt, k_sample, v_sample,
          lru_conv_prompt, lru_conv_sample, lru_h_prompt, lru_h_sample,
          ffn_conv_prompt, ffn_conv_sample):
    ctx = ExitStack()
    temps = ExitStack()

    def sb(name, shape, dt=F32):
        return ctx.enter_context(nc.sbuf_tensor(name, shape, dt))

    def tmp(name, shape, dt=F32):
        return temps.enter_context(nc.sbuf_tensor(name, shape, dt))

    names = {}

    def sem(name):
        if name not in names:
            names[name] = ctx.enter_context(nc.semaphore(name))
        return names[name]

    x_save = nc.dram_tensor("x_save", (P, KT * T), F32, kind="Internal").ap()

    with ctx:
        act_hi = sb("act_hi", [P, KT, T], F32R)
        act_lo = sb("act_lo", [P, KT, T], F32R)
        X = sb("X", [P, KT, T])
        raw = [sb(f"raw{s}", [P, KB, P]) for s in range(SLOTS)]
        w_hi = [sb(f"w_hi{s}", [P, KB, P], F32R) for s in range(SLOTS)]
        w_lo = [sb(f"w_lo{s}", [P, KB, P], F32R) for s in range(SLOTS)]
        vec = sb("vec", [P, 640])
        mod = sb("mod", [P, NM, CB])
        ident = sb("ident", [P, P])
        neg_later = sb("neg_later", [P, P])
        neg_ones = sb("neg_ones", [P, P])
        before = sb("before", [P, P])
        cs = sb("cs", [P, KT, 2 * CB], F32R)
        eps = sb("eps", [P, 1])
        sel = sb("sel", [2 * CB, CB])
        mod_rows = sb("mod_rows", [2 * CB, 4, P])
        lst = sb("lst", [P, 256])
        lnew = sb("lnew", [P, 288])
        bias_h = sb("bias_h", [P, NH])
        c8 = sb("c8", [P, 2, NL])
        same = sb("same", [SAMP, SAMP])
        xr = tmp("xr", [P, 5, D])
        vr = tmp("vr", [P, 5, P])
        lsr = tmp("lsr", [P, 2, P])
        sq = tmp("sq", [P, 2, T])
        rs = tmp("rs", [P, T])
        temps.close()
        xr_flat = xr[:].rearrange("p a b -> p (a b)")
        mod_t = xr_flat[:, 0:1024]
        mod_u = xr_flat[:, 1024:2048]
        s1 = xr_flat[:, 2048:2048 + KT * CB].rearrange("p (k c) -> p k c", c=CB)
        hp = [xr_flat[:, 3072 + 512 * i:3584 + 512 * i] for i in range(2)]
        qs = tmp("qs", [P, NH, SAMP])
        vs = tmp("vs", [SAMP, NH, P])
        zs = tmp("zs", [P, NH, SAMP])
        mark = temps.pop_all()
        qraw = tmp("qraw", [P, T])
        kraw = tmp("kraw", [P, T])
        qf = tmp("qf", [P, T])
        kf = tmp("kf", [P, T])
        vf = tmp("vf", [P, T])
        sqq = tmp("sqq", [P, T])
        sqk = tmp("sqk", [P, T])
        zf = tmp("zf", [P, 1280])
        sp_ = tmp("sp_", [P, 1280])
        wt = tmp("wt", [P, 1280])
        vn = tmp("vn", [P, 4, P])
        kn = tmp("kn", [P, 4, P])
        ksn = tmp("ksn", [SAMP, P])
        temps.close()
        kpg = [tmp(f"kpg{i}", [P, NH, P]) for i in range(2)]
        vpg = [tmp(f"vpg{i}", [P, NH, P]) for i in range(2)]
        kt_ = [tmp(f"kt{i}", [P, 4, P]) for i in range(2)]
        zc = tmp("zc", [P, 512])
        wself = tmp("wself", [SAMP, 512])
        spc = tmp("spc", [P, 512])
        suf = tmp("suf", [P, 512])
        xlp = tmp("xlp", [P, 3 + SEQ + NB * 11])
        xc = tmp("xc", [P, T])
        La = tmp("La", [P, T])
        Lb = tmp("Lb", [P, T])
        Lc = tmp("Lc", [P, T])
        gg = tmp("gg", [P, T])
        wg = tmp("wg", [P, 2, P])
        pt = tmp("pt", [1, 64], I32)
        temps.close()
        mark.close()
        cv = tmp("cv", [P, 18, NM])
        crl = tmp("crl", [P, 3 * P])
        mark2 = temps.pop_all()
        str_ = tmp("str_", [P, 12, P])
        sq2 = tmp("sq2", [P, 2, T])
        xres = tmp("xres", [P, 2, T])
        hp2 = tmp("hp2", [P, 2, SEQ])
        mt2 = tmp("mt2", [P, 2, 1024])
        rs2 = tmp("rs2", [P, T])
        s2 = tmp("s2", [P, KT, CB])
        t64 = tmp("t64", [P, 2, SAMP])
        temps.close()
        g_hi = tmp("g_hi", [P, G, T], F32R)
        g_lo = tmp("g_lo", [P, G, T], F32R)
        up = [tmp(f"up{i}", [P, 2 + SEQ + NB * 10]) for i in range(2)]
        uc = [tmp(f"uc{i}", [P, T]) for i in range(2)]
        gp = tmp("gp", [P, T])
        t64b = tmp("t64b", [P, 2, SAMP])
        temps.close()
        yr = tmp("yr", [P, 2, D])
        crt = tmp("crt", [P, 14, P])
        temps.close()
        mark2.close()

        ps = ctx.enter_context(nc.psum_tensor("ps", [P, 8, 512], F32))
        gps = [ps[:, 0:2, 0:HALF], ps[:, 2:4, 0:HALF]]

        def flat2(a):
            return a.rearrange("p (h n) -> p h n", h=2)

        xlp_s = xlp[:, 3 + SEQ:].rearrange("p (b t) -> p b t", t=11)
        up_s = [u[:, 2 + SEQ:].rearrange("p (b t) -> p b t", t=10) for u in up]

        s_raw = [sem(f"raw_loaded{s}") for s in range(SLOTS)]
        hi_done, lo_done, blk_used = sem("hi_done"), sem("lo_done"), sem("block_used")

        wi_v = w_in[0].rearrange("(k p) n -> p k n", p=P)
        wa_v = w_ada[0].rearrange("(k p) n -> p k n", p=P)
        wo_v = w_out[0].rearrange("(k p) n -> p k n", p=P)
        wu_v = w_up[0].rearrange("(k p) n -> p k n", p=P)
        wd_v = w_down[0].rearrange("(k p) n -> p k n", p=P)

        block = ctx.enter_context(nc.Block())

        @block.sync
        def _(sp):
            def load(u, k, view, row, nk, col):
                wait(sp, lo_done, u[0] + (k - SLOTS + 1))
                sp.dma_start(raw[k % SLOTS][:, 0:nk, :],
                             view[:, bass.ds(row, nk), bass.ds(col, P)]).then_inc(s_raw[k % SLOTS], 16)

            def tile(u, k, view, col):
                for h in range(2):
                    load(u, k + h, view, h * KB, KB, col)

            cflat = X[:].rearrange("p k n -> p (k n)")
            c_loaded = sem("c_loaded")
            sp.wait_ge(sem("zeroed"), 2)
            sp.dma_start(cflat[0:8, 0:D], c_sample).then_inc(c_loaded, 16)
            sp.dma_start(cflat[8:9, 0:D], c_prompt).then_inc(c_loaded, 16)
            vecs = sem("vecs_loaded")

            def rows(t, p0, n, src):
                sp.dma_start(vr[p0:p0 + n, t, :], src).then_inc(vecs, 16)
            rows(0, 0, 96, b_ada.rearrange("a (r c) -> (a r) c", c=P))
            rows(0, 96, 16, g_norm1.rearrange("a (r c) -> (a r) c", c=P))
            rows(0, 112, 16, g_norm2.rearrange("a (r c) -> (a r) c", c=P))
            rows(1, 0, 32, w_lru_conv.rearrange("a w (r c) -> (a w r) c", c=P))
            rows(1, 32, 8, b_lru_conv.rearrange("a (r c) -> (a r) c", c=P))
            rows(1, 40, 8, b_lru_a.rearrange("a r c -> (a r) c"))
            rows(1, 48, 8, b_lru_x.rearrange("a r c -> (a r) c"))
            rows(1, 56, 8, lru_lambda.rearrange("a (r c) -> (a r) c", c=P))
            rows(1, 64, 1, g_q)
            rows(1, 65, 1, g_k)
            fw = w_ffn_conv.rearrange("a w (r c) -> (a w r) c", c=P)
            rows(2, 0, 128, fw[0:128])
            rows(3, 0, 128, fw[128:256])
            rows(4, 0, 32, fw[256:288])
            rows(4, 32, 96, b_ffn_conv.rearrange("a (r c) -> (a r) c", c=P))
            st = state_lru_conv.rearrange("a b w (r c) -> (a b w r) c", c=P)
            sp.dma_start(lsr[:, 0, :], st[0:128]).then_inc(vecs, 16)
            sp.dma_start(lsr[0:64, 1, :], st[128:192]).then_inc(vecs, 16)
            sp.dma_start(lsr[64:128, 1, :], state_lru_h.rearrange("a b (r c) -> (a b r) c", c=P)).then_inc(vecs, 16)
            x_loaded = sem("x_loaded")
            for t in range(4):
                sp.dma_start(xr[:, t, :], x_prompt[0, t * P:(t + 1) * P, :]).then_inc(x_loaded, 16)
            sp.dma_start(xr[0:SAMP, 4, :], x_sample.rearrange("b t d -> (b t) d")).then_inc(x_loaded, 16)

            def ada(i):
                u = turn(B_ADA, i, 8)
                for j in range(4):
                    tile(u, 2 * j, wa_v, 512 * i + 128 * j)
            turns(sp, 8, ada)

            def qkv(i):
                u = turn(B_QKV, i, 8)
                tile(u, 0, wi_v, 128 * i)
                tile(u, 2, wa_v, 128 * i + 32 * 128)
                tile(u, 4, wi_v, 128 * i + 1024)
                tile(u, 6, wi_v, 128 * i + 2048)
            turns(sp, NH, qkv)

            def lru(i):
                u = turn(B_LRU, i, 16)
                for q in range(4):
                    load(u, 4 * q, wi_v, (q % 2) * KB, KB, 128 * i + (3072, 4096)[q // 2])
                    for r in range(3):
                        n = 3 * q + r
                        load(u, 4 * q + 1 + r, wa_v, (n % 2) * KB, KB, 768 * i + (40 + n // 2) * 128)
            turns(sp, NL, lru)

            def out(i):
                u = turn(B_OUT, i, 12)
                for j in range(4):
                    tile(u, (0, 2, 6, 8)[j], wo_v, 512 * i + 128 * j)
                    if j % 2:
                        tile(u, (4, 10)[j // 2], wa_v, 256 * i + (88 + j // 2) * 128)
            turns(sp, 4, out)

            with sp.Fori(0, NG) as g:
                with sp.Fori(0, G) as j:
                    u = ffn_up(g, j)
                    tile(u, 0, wu_v, 768 * g + 128 * j)
                    tile(u, 2, wu_v, 768 * g + 128 * j + NFF * P)
                with sp.Fori(0, 4) as m:
                    u = ffn_down(g, m)
                    for c in range(4):
                        load(u, c, wd_v, G * g, G, 512 * m + 128 * c)

            for t in range(5):
                sp.wait_ge(sem("y_even"), 2 * t + 2)
                sp.wait_ge(sem("y_odd"), 2 * t + 2)
                dst = y_prompt[0, t * P:(t + 1) * P, :] if t < 4 else y_sample.rearrange("b t d -> (b t) d")
                sp.dma_start(dst, yr[0:P if t < 4 else SAMP, t % 2, :]).then_inc(sem(f"y_stored{t % 2}"), 16)
            sp.wait_ge(sem("y_stored0"), 48)
            sp.wait_ge(sem("y_stored1"), 32)

        @block.tensor
        def _(pe):
            def ready(u, k):
                pe.wait_ge(lo_done, u[0] + (k + 1))

            def product(u, k, out, hi, lo, nk=KB, first=True, last=True, k0=0, each=None,
                        between=None):
                ready(u, k)
                s = k % SLOTS
                for kk in range(nk):
                    if between is not None:
                        between(kk)
                    if each is not None:
                        pe.wait_ge(each, k0 + kk + 1)
                    for w, xs in ((w_hi, (hi, lo)), (w_lo, (hi,))):
                        for x in xs:
                            for h in range(2):
                                mm = pe.matmul(out[:, h, :], w[s][:, kk, :], x[:, k0 + kk, h * HALF:(h + 1) * HALF],
                                               start=first and kk == 0 and w is w_hi and x is hi,
                                               stop=last and kk == nk - 1 and w is w_lo)
                mm.then_inc(blk_used, 1)
                return mm

            def ada_block(u, k, j, h):
                ready(u, k)
                for kk in range(KB):
                    for w in (w_hi, w_lo):
                        mm = pe.matmul(ps[0:2 * CB, 4, P * j:P * (j + 1)], cs[:, h * KB + kk, :], w[k % SLOTS][:, kk, :],
                                       start=h == 0 and kk == 0 and w is w_hi,
                                       stop=h == 1 and kk == KB - 1 and w is w_lo)
                mm.then_inc(blk_used, 1)

            def ada_chunk(u, k, j):
                for h in range(2):
                    ada_block(u, k + h, j, h)

            def turn_mod(n, t):
                pe.wait_ge(sem("rows_taken"), t + 1)
                for j in range(n):
                    mm = pe.matmul(ps[:, 4, 448 + CB * j:448 + CB * (j + 1)], mod_rows[:, j, :], sel[:], start=True, stop=True)
                mm.then_inc(sem("mod_turned"), 1)

            pe.wait_ge(sem("consts"), 1)
            pe.wait_ge(sem("silu"), 1)
            cflat = X[:].rearrange("p k n -> p (k n)")
            for k in range(KT):
                mm = pe.transpose(ps[:, 0, CB * k:CB * k + CB], cflat[0:CB, D + k * P:D + (k + 1) * P], ident[0:CB, 0:CB])
            mm.then_inc(sem("c_turned"), 1)
            pe.wait_ge(sem("vecs_loaded"), 16 * 17)
            pe.wait_ge(sem("zeroed"), 2)
            for t in range(5):
                pe.transpose(ps[:, 1 + t // 4, (t % 4) * P:(t % 4 + 1) * P], vr[:, t, :], ident[:])
            for t in range(2):
                mm = pe.transpose(ps[:, 3, t * P:(t + 1) * P], lsr[:, t, :], ident[:])
            mm.then_inc(sem("vecs_turned"), 1)
            pe.wait_ge(sem("x_loaded"), 80)
            pe.wait_ge(sem("c_taken"), 1)
            pe.wait_ge(sem("vecs_taken"), 3)
            XB = ((5, 7), (6, 3))

            def squares(k, first, last, ready_sem):
                pe.wait_ge(ready_sem, k + 1)
                for h in range(2):
                    mm = pe.matmul(ps[:, 1 + h, 0:HALF], neg_ones[:], sq[:, k % 2, h * HALF:(h + 1) * HALF],
                                   start=first, stop=last)
                mm.then_inc(sem("squares_used"), 1)

            for k in range(KT):
                if k >= 2:
                    pe.wait_ge(sem("x_taken_p"), k - 1)
                    pe.wait_ge(sem("x_taken_s"), k - 1)
                bp, bs = XB[k % 2]
                for t in range(4):
                    pe.transpose(ps[:, bp, t * P:(t + 1) * P], xr[:, t, k * P:(k + 1) * P], ident[:])
                pe.transpose(ps[:, bs, 0:SAMP], xr[0:SAMP, 4, k * P:(k + 1) * P], ident[0:SAMP, 0:SAMP]).then_inc(sem("x_turned"), 1)
                if k:
                    squares(k - 1, k == 1, False, sem("sq_ready"))
            squares(KT - 1, False, True, sem("sq_ready"))

            for kk in (KT - 1,):
                pe.wait_ge(sem("x_taken_p"), kk + 1)
                pe.wait_ge(sem("x_taken_s"), kk + 1)

            def ada(i):
                u = turn(B_ADA, i, 8)
                wait(pe, sem("bank4_taken"), i)
                for j in range(4):
                    ada_chunk(u, 2 * j, j)
                turn_mod(4, i)
            turns(pe, 8, ada)

            def scores(i):
                pe.wait_ge(sem("qk_ready"), i)
                pe.wait_ge(sem("rk_taken"), i)
                wait(pe, sem("o_taken"), i - 1)
                for j in range(4):
                    b, c = ZB[j]
                    pe.matmul(ps[:, b, c:c + QW[j]], kf[:, j * P:(j + 1) * P], qf[:, j * P:SEQ], start=True, stop=True)
                pe.matmul(ps[0:SAMP, 4, 384:384 + SAMP], kf[:, SEQ:T], qf[:, SEQ:T], start=True, stop=True) \
                  .then_inc(sem("scores_mm"), 1)

            def sums(i):
                pe.wait_ge(sem("sp_ready"), i)
                for j in range(4):
                    b, c = ZB[j]
                    mm = pe.matmul(ps[:, b, c:c + QW[j]], neg_later[:], sp_[:, J0[j]:J0[j] + QW[j]],
                                   start=True, stop=j == 3)
                    for jj in range(j + 1, 4):
                        c2 = c + (jj - j) * P
                        mm = pe.matmul(ps[:, b, c2:c2 + QW[jj]], neg_ones[:], sp_[:, J0[jj]:J0[jj] + QW[jj]],
                                       start=False, stop=jj == 3)
                mm.then_inc(sem("sums_mm"), 1)

            def turn_kv(i):
                for t in range(4):
                    pe.transpose(ps[:, 2, t * P:(t + 1) * P], vf[:, t * P:(t + 1) * P], ident[:])
                for t in range(4):
                    pe.transpose(ps[:, 3, t * P:(t + 1) * P], kf[:, t * P:(t + 1) * P], ident[:])
                pe.transpose(ps[0:SAMP, 4, 128:256], vf[:, SEQ:T], ident[:])
                pe.transpose(ps[0:SAMP, 4, 256:384], kf[:, SEQ:T], ident[:]).then_inc(sem("kv_turned"), 1)

            def weigh(i):
                pe.wait_ge(sem("w_ready"), i)
                pe.wait_ge(sem("vn_taken"), i)
                for j in range(4):
                    mm = pe.matmul(ps[:, 7, j * P:SEQ], vn[:, j, :], wt[:, J0[j]:J0[j] + QW[j]],
                                   start=j == 0, stop=j == 3)
                mm.then_inc(sem("o_mm"), 1)

            def head_squares(b0, src, out_sem):
                for h in range(2):
                    mm = pe.matmul(ps[:, b0 + h, 0:HALF], neg_ones[:], src[:, h * HALF:(h + 1) * HALF],
                                   start=True, stop=True)
                mm.then_inc(out_sem, 1)

            def qkv(i):
                u = turn(B_QKV, i, 8)
                first = starts(i)
                wait(pe, sem("v_out"), i)
                each = sem("x1_ready") if first else None
                product(u, 0, gps[0], act_hi, act_lo, last=False, each=each)
                product(u, 1, gps[0], act_hi, act_lo, first=False, k0=KB, each=each)
                pe.wait_ge(sem("bank4_taken"), i + 8)
                ada_chunk(u, 2, 0)
                if not first:
                    scores(i)
                wait(pe, sem("rq_taken"), i)
                product(u, 4, gps[1], act_hi, act_lo, last=False)
                product(u, 5, gps[1], act_hi, act_lo, first=False, k0=KB)
                if not first:
                    sums(i)
                pe.wait_ge(sem("q_out"), 2 * i + 2)
                product(u, 6, gps[0], act_hi, act_lo, last=False)
                turn_mod(1, i + 8)
                pe.wait_ge(sem("k_out"), 2 * i + 2)
                if not first:
                    turn_kv(i)
                product(u, 7, gps[0], act_hi, act_lo, first=False, k0=KB)
                if not first:
                    weigh(i)
                    pe.wait_ge(sem("kn_taken"), i)
                head_squares(2, sqq, sem("ssq_mm"))
                head_squares(5, sqk, sem("ssk_mm"))
            turns(pe, NH, qkv, 2)

            pe.wait_ge(sem("bank4_taken"), 16)
            pe.wait_ge(sem("rq_taken"), NH)
            scores(NH)
            sums(NH)
            turn_kv(NH)
            weigh(NH)
            pe.wait_ge(sem("o_taken"), NH)
            pe.wait_ge(sem("self_sp_ready"), 1)
            pe.matmul(ps[0:SAMP, 7, :], neg_later[0:SAMP, 0:SAMP], zs[0:SAMP].rearrange("p h q -> p (h q)"),
                      start=True, stop=True).then_inc(sem("self_mm"), 1)
            pe.wait_ge(sem("self_done"), 1)

            def turn_k(i, h):
                s = h // 2
                if h % 2 == 0:
                    pe.wait_ge(sem(f"k_loaded{s % 2}"), 64 * i + 16 * (s // 2 + 1))
                if h:
                    pe.wait_ge(sem("kb_taken" if h % 2 == 0 else "ka_taken"), 8 * i + (h + 1) // 2)
                else:
                    wait(pe, sem("kb_taken"), 8 * i)
                for n in range(4):
                    mm = pe.transpose(ps[:, 5, n * P:(n + 1) * P], kpg[s % 2][:, 4 * (h % 2) + n, :], ident[:])
                mm.then_inc(sem("kb_turned" if h % 2 else "ka_turned"), 1)

            def score_k(i, h):
                s, a = h // 2, h % 2
                pe.wait_ge(sem("kb_taken" if a else "ka_taken"), 8 * i + s + 1)
                if h == 0:
                    wait(pe, sem("zc_taken"), i)
                for n in range(4):
                    c = s * 64 + (4 * a + n) * NS
                    mm = pe.matmul(ps[:, 7, c:c + NS], kt_[a][:, n, :], qs[:, 4 * a + n, bass.ds(8 * i, NS)],
                                   start=True, stop=True)
                mm.then_inc(sem("kb_used" if a else "ka_used"), 1)

            def page_sums(i):
                pe.wait_ge(sem("spc_ready"), i)
                wait(pe, sem("o2_taken"), i - 1)
                pe.matmul(ps[:, 6, :], neg_later[:], spc[:], start=True, stop=False)
                pe.matmul(ps[:, 6, :], neg_ones[:], suf[:], start=False, stop=True).then_inc(sem("sums2_mm"), 1)

            def weigh_page(i, s):
                if s == 0:
                    pe.wait_ge(sem("wc_ready"), i)
                pe.wait_ge(sem(f"v_loaded{s % 2}"), 64 * i + (16 * (s // 2 + 1) - 64))
                for h in range(NH):
                    mm = pe.matmul(ps[:, 6, h * NS:(h + 1) * NS], vpg[s % 2][:, h, :],
                                   suf[:, s * 64 + h * NS:s * 64 + (h + 1) * NS],
                                   start=s == 0 and h == 0, stop=False, skip_group_check=True)
                mm.then_inc(sem("v_used"), 1)
                if s == PAGES - 1:
                    for h in range(NH):
                        mm = pe.matmul(ps[:, 6, h * NS:(h + 1) * NS], vs[:, h, :],
                                       wself[:, bass.ds(8 * i + (h * SAMP - 8), NS)],
                                       start=False, stop=True, skip_group_check=True)
                    mm.then_inc(sem("o2_mm"), 1)

            def gate(i, which, out_sem):
                for h in range(2):
                    mm = pe.matmul(ps[:, h, 0:HALF], wg[:, which, :], xc[:, h * HALF:(h + 1) * HALF], start=True, stop=True)
                mm.then_inc(sem(out_sem), 1)

            def lru(i):
                u, prev = turn(B_LRU, i, 16), not starts(i)

                def between(q):
                    def f(kk):
                        t = 8 * q + kk
                        if t % 2 == 0:
                            turn_k(i, t // 2)
                        elif t >= 3:
                            score_k(i, (t - 3) // 2)
                        if t == 2:
                            turn_mod(3, 2 * i + 15) if prev else None
                        if t == 18:
                            turn_mod(3, 2 * i + 16)
                        if prev and t == 6:
                            page_sums(i)
                        if prev and t >= 9 and t % 3 == 0:
                            weigh_page(i, (t - 9) // 3)
                        if t == 28:
                            pe.wait_ge(sem("gates_loaded"), 32 * i + 32)
                            pe.wait_ge(sem("xc_ready"), i + 1)
                            gate(i, 0, "r_mm")
                    return f

                wait(pe, sem("i_taken"), i)
                for q in range(4):
                    if q == 2:
                        wait(pe, sem("gl_out"), i)
                    product(u, 4 * q, gps[q // 2], act_hi, act_lo, first=q % 2 == 0, last=q % 2 == 1, k0=KB * (q % 2),
                            between=between(q))
                    if q % 2 == 0:
                        pe.wait_ge(sem("bank4_taken"), 2 * i + 17 + q // 2)
                    for r in range(3):
                        n = 3 * q + r
                        ada_block(u, 4 * q + 1 + r, (n // 2) % 3, n % 2)
                        if q == 3 and r == 0:
                            score_k(i, 15)
                pe.wait_ge(sem("r_taken"), i + 1)
                gate(i, 1, "i_mm")
            turns(pe, NL, lru, 2)
            turn_mod(3, 31)
            page_sums(NL)
            for s in range(PAGES):
                weigh_page(NL, s)

            def sum2(m, slot, first, last):
                pe.wait_ge(sem("sq2_ready"), m + 1)
                for h in range(2):
                    mm = pe.matmul(ps[:, 5 + h, 0:HALF], neg_ones[:], sq2[:, slot, h * HALF:(h + 1) * HALF],
                                   start=first, stop=last)
                mm.then_inc(sem("sq2_used"), 1)

            def out(i):
                u = turn(B_OUT, i, 12)
                first = isinstance(i, int)
                for j in range(4):
                    wait(pe, sem("x2_ready"), 4 * i + (j - 1))
                    if first and j == 0:
                        pe.wait_ge(sem("i_taken"), NL)
                    if first and j == 1:
                        pe.wait_ge(sem("gl_out"), NL)
                    k = (0, 2, 6, 8)[j]
                    each = sem("mix_ready") if first and j == 0 else None
                    product(u, k, gps[j % 2], act_hi, act_lo, last=False, each=each)
                    product(u, k + 1, gps[j % 2], act_hi, act_lo, first=False, k0=KB, each=each)
                    if j % 2:
                        if j == 1:
                            pe.wait_ge(sem("bank4_taken"), i + 33)
                        ada_chunk(u, k + 2, j // 2)
                    if not first or j:
                        sum2(4 * i + (j - 1), (j + 1) % 2, first and j == 1, False)
                turn_mod(2, i + 32)
            turns(pe, 4, out)
            sum2(KT - 1, 1, False, True)
            pe.wait_ge(sem("ffn_state_loaded"), 16)
            pe.wait_ge(sem("x2_ready"), KT)
            pe.wait_ge(sem("bank4_taken"), 37)
            for t in range(12):
                mm = pe.transpose(ps[:, (7, 4, 3)[t // 4], (t % 4) * P:(t % 4 + 1) * P], str_[:, t, :], ident[:])
            mm.then_inc(sem("ffn_state_turned"), 1)
            for t, n in ((0, P), (1, P), (2, 32)):
                mm = pe.transpose(ps[0:n, 2, t * P:(t + 1) * P], lnew[:, t * P:t * P + n], ident[:])
            mm.then_inc(sem("lnew_turned"), 1)

            def up_tile(g, j, each=None):
                u, nt = ffn_up(g, j), G * g + j
                wait(pe, sem("gate_out"), 3 * nt)
                if not isinstance(g, int) or g:
                    pe.wait_ge(sem("y_taken"), KT * g)
                product(u, 0, gps[0], act_hi, act_lo, last=False, each=each)
                product(u, 1, gps[0], act_hi, act_lo, first=False, k0=KB, each=each)
                if each is not None:
                    pe.wait_ge(sem("cv_taken"), 3)
                    pe.wait_ge(sem("lnew_taken"), 2)
                wait(pe, sem("value_out"), 3 * nt)
                product(u, 2, gps[1], act_hi, act_lo, last=False)
                product(u, 3, gps[1], act_hi, act_lo, first=False, k0=KB)

            def down(g):
                pe.wait_ge(sem("gate_out"), 3 * G * g + 3 * G)
                pe.wait_ge(sem("value_out"), 3 * G * g + 3 * G)
                pe.wait_ge(sem("g_ready"), G * g + G)

                def four(m):
                    u = ffn_down(g, m)
                    for c in range(4):
                        if not isinstance(m, int) or m or c >= 2:
                            pe.wait_ge(sem("y_taken"), KT * g + 4 * m + c - 1)
                        product(u, c, gps[c % 2], g_hi, g_lo, nk=G)
                four(0)
                with pe.Fori(1, 4) as m:
                    four(m)

            up_tile(0, 0, each=sem("x3_ready"))
            with pe.Fori(1, G) as j:
                up_tile(0, j)
            down(0)
            with pe.Fori(1, NG) as g:
                with pe.Fori(0, G) as j:
                    up_tile(g, j)
                down(g)

            pe.wait_ge(sem("y_taken"), KT * NG)
            pe.wait_ge(sem("cv_saved"), 4 * NFF)
            n = 0
            for t in range(5):
                w = P if t < 4 else SAMP
                for q in range(4):
                    if n >= 8:
                        pe.wait_ge(sem("y_odd" if n % 2 else "y_even"), (n - 8) // 2 + 1)
                    for k in range(4):
                        mm = pe.transpose(ps[0:w, n % 8, k * P:(k + 1) * P], X[:, 4 * q + k, t * P:t * P + w], ident[:])
                    mm.then_inc(sem("y_turned"), 1)
                    n += 1
            cvf = cv[:].rearrange("p r m -> p (r m)")
            for q in range(4):
                pe.wait_ge(sem("y_odd" if n % 2 else "y_even"), (n - 8) // 2 + 1)
                for k in range(4):
                    t = 4 * q + k
                    if t < 14:
                        w = min(P, 18 * NM - t * P)
                        mm = pe.transpose(ps[0:w, n % 8, k * P:(k + 1) * P], cvf[:, t * P:t * P + w], ident[:])
                mm.then_inc(sem("y_turned"), 1)
                n += 1

        @block.scalar
        def _(act):
            ch = Chain(act, sem("act_steps"))

            def hi(u, k):
                s = k % SLOTS
                wait(act, blk_used, u[0] + (k - SLOTS + 1))
                act.wait_ge(s_raw[s], 16 * u[1] + 16 * (k // SLOTS + 1))
                act.activation(w_hi[s][:], raw[s][:], ACT.Copy).then_inc(hi_done, 1)

            def used(u, k):
                act.wait_ge(blk_used, u[0] + k)

            act.wait_ge(sem("c_loaded"), 32)
            cflat = X[:].rearrange("p k n -> p (k n)")
            act.activation(cflat[0:CB, D:2 * D], cflat[0:CB, 0:D], ACT.Silu).then_inc(sem("silu"), 1)
            act.wait_ge(sem("c_turned"), 1)
            act.activation(cs[:, :, 0:CB], ps[:, 0, 0:KT * CB].rearrange("p (k c) -> p k c", c=CB), ACT.Copy) \
               .then_inc(sem("c_hi"), 1)
            act.wait_ge(sem("vecs_turned"), 1)
            act.activation(vec[:, 0:512], ps[:, 1, :], ACT.Copy).then_inc(sem("vecs_taken"), 1)
            act.activation(vec[:, 512:640], ps[:, 2, 0:P], ACT.Copy).then_inc(sem("vecs_taken"), 1)
            u = turn(B_ADA, 0, 8)
            for k in range(SLOTS):
                hi(u, k)
            act.wait_ge(sem("c_taken"), 1)
            for k in range(KT):
                act.wait_ge(sem("x_turned"), k + 1)
                act.activation(X[:, k, 0:SEQ], ps[:, 5 + k % 2, :], ACT.Copy).then_inc(sem("x_taken_p"), 1)
                act.wait_ge(sem("x_taken_p"), k + 1)
                act.wait_ge(sem("x_taken_s"), k + 1)
                if k >= 2:
                    act.wait_ge(sem("squares_used"), k - 1)
                act.activation(sq[:, k % 2, :], X[:, k, :], ACT.Square).then_inc(sem("sq_ready"), 1)
            act.dma_start(x_save, X[:].rearrange("p k n -> p (k n)")).then_inc(sem("x_saved"), 16)
            act.wait_ge(sem("squares_used"), KT)
            ch.enter(0, 1)
            ch.link(act.activation(flat2(rs[:]), ps[:, 1:3, 0:HALF], ACT.Ln, bias=eps[:], scale=-1.0 / D))
            act.activation(rs[:], rs[:], ACT.Exp, scale=-0.5).then_inc(sem("rs_ready"), 1)
            ch.advance(1)

            def ada(i):
                u = turn(B_ADA, i, 8)
                for k in range(8):
                    hi(u, k + SLOTS)
            turns(act, 8, ada)

            for k in range(KT):
                act.wait_ge(sem("hp_ready"), k + 1)
                act.activation(act_hi[:, k, 0:SEQ], hp[k % 2], ACT.Identity, bias=mod[:, k, 8:9]).then_inc(sem("x1_hi"), 1)
                if k == 0:
                    act.wait_ge(sem("hs_ready"), 1)
                    act.activation(act_hi[:, :, SEQ:T], mod_t.rearrange("p (k n) -> p k n", n=SAMP), ACT.Copy) \
                       .then_inc(sem("x1_hi_s"), 1)

            act.wait_ge(sem("vecs_taken"), 3)
            act.wait_ge(sem("x_saved"), 16)
            def softplus_part(i):
                act.wait_ge(sem("z_taken"), i)
                ch.link(act.activation(wt[:], zf[:], ACT.Abs))
                ch.link(act.activation(wt[:], wt[:], ACT.Exp, scale=-1.0))
                act.activation(wt[:], wt[:], ACT.Ln, bias=1.0).then_inc(sem("lz_ready"), 1)

            def weights(i):
                act.wait_ge(sem("arg_ready"), i)
                act.activation(wt[:], zf[:], ACT.Exp).then_inc(sem("w_exp"), 1)

            def take_v(i):
                act.wait_ge(sem("kv_turned"), i)
                wait(act, sem("o_mm"), i - 1)
                wait(act, sem("v_stored"), 16 * i - 16)
                act.activation(vn[:], ps[:, 2, :].rearrange("p (t d) -> p t d", d=P), ACT.Copy).then_inc(sem("vn_taken"), 1)

            def take_o(i):
                act.wait_ge(sem("o_mm"), i)
                act.activation(X[:, bass.ds(i - 1, 1), 0:SEQ].rearrange("p a n -> p (a n)"), ps[:, 7, :], ACT.Copy).then_inc(sem("o_taken"), 1)

            def qkv(i):
                u, prev = turn(B_QKV, i, 8), not starts(i)
                hi(u, 4)
                hi(u, 5)
                used(u, 2)
                wait(act, sem("qk_ready"), i)
                act.activation(flat2(sqq[:]), gps[0], ACT.Square).then_inc(sem("q_out"), 1)
                act.activation(flat2(qraw[:]), gps[0], ACT.Copy).then_inc(sem("q_out"), 1)
                hi(u, 6)
                hi(u, 7)
                if prev:
                    ch.enter(2 * i - 2, 2)
                    softplus_part(i)
                    ch.leave()
                hi(u, 8)
                hi(u, 9)
                used(u, 6)
                act.activation(flat2(sqk[:]), gps[1], ACT.Square).then_inc(sem("k_out"), 1)
                act.activation(flat2(kraw[:]), gps[1], ACT.Copy).then_inc(sem("k_out"), 1)
                if prev:
                    weights(i)
                hi(u, 10)
                if prev:
                    take_v(i)
                hi(u, 11)
                used(u, 8)
                act.activation(flat2(vf[:]), gps[0], ACT.Copy).then_inc(sem("v_out"), 1)
                if prev:
                    take_o(i)
                for src, b0, mm, rd, done in ((sqq, 2, "ssq_mm", "rq_taken", "rq_ready"),
                                              (sqk, 5, "ssk_mm", "rk_taken", "rk_ready")):
                    act.wait_ge(sem(mm), i + 1)
                    act.activation(flat2(src[:]), ps[:, b0:b0 + 2, 0:HALF], ACT.Ln, bias=eps[:], scale=-1.0 / P) \
                       .then_inc(sem(rd), 1)
                    act.wait_ge(sem(rd), i + 1)
                    act.activation(src[:], src[:], ACT.Exp, scale=-0.5).then_inc(sem(done), 1)
            turns(act, NH, qkv, 2)
            ch.advance(2 * NH - 2)
            ch.enter(0, 2)
            softplus_part(NH)
            ch.leave()
            ch.advance(2)
            weights(NH)
            take_v(NH)
            take_o(NH)

            zsf = zs[0:SAMP].rearrange("p h q -> p (h q)")
            ch.enter(0, 5)
            act.wait_ge(sem("self_z"), 1)
            ch.link(act.activation(wself[:], zsf, ACT.Abs))
            ch.link(act.activation(wself[:], wself[:], ACT.Exp, scale=-1.0))
            act.activation(wself[:], wself[:], ACT.Ln, bias=1.0).then_inc(sem("self_l"), 1)
            act.wait_ge(sem("self_arg"), 1)
            act.activation(wself[:], spc[0:SAMP, :], ACT.Exp).then_inc(sem("self_w"), 1)
            lam = vec[:, V_LAM:V_LAM + NL]
            ch.link(act.activation(c8[:, 0, :], lam, ACT.Abs))
            ch.link(act.activation(c8[:, 0, :], c8[:, 0, :], ACT.Exp, scale=-1.0))
            ch.link(act.activation(c8[:, 0, :], c8[:, 0, :], ACT.Ln, bias=1.0))
            ch.leave()
            ch.advance(5)
            act.activation(c8[:, 1, :], lam, ACT.Relu, scale=-1.0).then_inc(sem("c8_parts"), 1)

            def coefficients(i):
                act.wait_ge(sem("c8_ready"), 1)
                act.wait_ge(sem("r_taken"), i)
                act.wait_ge(sem("lnew_saved"), 2 * i)
                act.wait_ge(sem("xc_ready"), i)
                act.activation(Lc[:], La[:], ACT.Exp, scale=c8[:, 0, bass.ds(i - 1, 1)]).then_inc(sem("a_ready"), 1)
                act.activation(xlp[:, 3:3 + T], La[:], ACT.Tanh, scale=c8[:, 1, bass.ds(i - 1, 1)]).then_inc(sem("a_ready"), 1)

            def root(i):
                act.wait_ge(sem("m2_ready"), i)
                act.activation(xlp[:, 3:3 + T], xlp[:, 3:3 + T], ACT.Sqrt).then_inc(sem("m_ready"), 1)

            def softplus_pages(i):
                act.wait_ge(sem("zc_taken"), i)
                ch.link(act.activation(spc[:], zc[:], ACT.Abs))
                ch.link(act.activation(spc[:], spc[:], ACT.Exp, scale=-1.0))
                act.activation(spc[:], spc[:], ACT.Ln, bias=1.0).then_inc(sem("lc_ready"), 1)

            def page_weights(i):
                act.wait_ge(sem("argc_ready"), i)
                act.activation(suf[:], zc[:], ACT.Exp).then_inc(sem("wc_ready"), 1)

            def take_o2(i):
                act.wait_ge(sem("o2_mm"), i)
                act.activation(X[:, 0:NH, bass.ds(NS * i + (SEQ - NS), NS)], ps[:, 6, 0:NH * NS].rearrange("p (h q) -> p h q", q=NS),
                               ACT.Copy).then_inc(sem("o2_taken"), 1)

            def take_keys(i, s):
                act.wait_ge(sem("ka_turned"), 8 * i + (s + 1))
                wait(act, sem("ka_used"), 8 * i + s)
                act.activation(kt_[0][:], ps[:, 5, :].rearrange("p (h k) -> p h k", k=P), ACT.Copy).then_inc(sem("ka_taken"), 1)

            def lru(i):
                u, prev = turn(B_LRU, i, 16), not starts(i)
                take_keys(i, 0)
                if prev:
                    ch.enter(2 * i - 2, 2)
                    softplus_pages(i)
                    ch.leave()
                take_keys(i, 1)
                if prev:
                    coefficients(i)
                for k in range(4, 8):
                    hi(u, k)
                take_keys(i, 2)
                if prev:
                    page_weights(i)
                    root(i)
                take_keys(i, 3)
                hi(u, 8)
                used(u, 5)
                wait(act, sem("lru_done"), i)
                act.activation(xlp[:, 3:3 + HALF], ps[:, 0, 0:HALF], ACT.Copy).then_inc(sem("xl_out"), 1)
                act.activation(xlp[:, 3 + HALF:3 + SEQ], ps[:, 1, 0:SEQ - HALF], ACT.Copy).then_inc(sem("xl_out"), 1)
                act.activation(xlp_s[:, :, 3:11], ps[:, 1, SEQ - HALF:HALF].rearrange("p (b t) -> p b t", t=NS), ACT.Copy) \
                   .then_inc(sem("xl_out"), 1)
                for k in range(9, 12):
                    hi(u, k)
                take_keys(i, 4)
                take_keys(i, 5)
                for k in range(12, 16):
                    hi(u, k)
                take_keys(i, 6)
                take_keys(i, 7)
                act.wait_ge(sem("r_mm"), i + 1)
                act.activation(flat2(La[:]), gps[0], ACT.Sigmoid, bias=vec[:, bass.ds(V_BA + i, 1)]).then_inc(sem("r_taken"), 1)
                hi(u, 16)
                used(u, 13)
                act.activation(flat2(gg[:]), gps[1], ACT.Gelu_apprx_tanh).then_inc(sem("gl_out"), 1)
                for k in range(17, 20):
                    hi(u, k)
                act.wait_ge(sem("i_mm"), i + 1)
                act.activation(flat2(Lb[:]), gps[0], ACT.Sigmoid, bias=vec[:, bass.ds(V_BX + i, 1)]).then_inc(sem("i_taken"), 1)
                if prev:
                    take_o2(i)
            turns(act, NL, lru, 2)
            ch.advance(2 * NL - 2)
            ch.enter(0, 2)
            softplus_pages(NL)
            ch.leave()
            ch.advance(2)
            coefficients(NL)
            page_weights(NL)
            root(NL)
            take_o2(NL)

            act.wait_ge(blk_used, B_OUT)
            act.wait_ge(sem("o_taken"), NH)
            act.wait_ge(sem("o2_taken"), NL)
            for k in range(KT):
                if k == KT - 1:
                    act.wait_ge(sem("lru_done"), NL)
                act.activation(act_hi[:, k, :], X[:, k, :], ACT.Copy).then_inc(sem("mix_hi"), 1)

            def out(i):
                u = turn(B_OUT, i, 12)
                for j in range(4):
                    k = (0, 2, 6, 8)[j]
                    hi(u, k + 4)
                    hi(u, k + 5)
                    if j % 2:
                        hi(u, k + 6)
                        hi(u, k + 7)
                    act.wait_ge(sem("x2_ready"), 4 * i + (j + 1))
                    wait(act, sem("sq2_used"), 4 * i + (j - 1))
                    act.activation(sq2[:, j % 2, :], X[:, bass.ds(4 * i + j, 1), :].rearrange("p a n -> p (a n)"), ACT.Square) \
                       .then_inc(sem("sq2_ready"), 1)
            turns(act, 4, out)
            act.wait_ge(sem("sq2_used"), KT)
            act.activation(flat2(rs2[:]), ps[:, 5:7, 0:HALF], ACT.Ln, bias=eps[:], scale=-1.0 / D).then_inc(sem("rs2_taken"), 1)
            act.wait_ge(sem("rs2_taken"), 1)
            act.activation(rs2[:], rs2[:], ACT.Exp, scale=-0.5).then_inc(sem("rs2_ready"), 1)
            act.wait_ge(sem("ffn_state_turned"), 1)
            for q in range(3):
                act.activation(cv[:].rearrange("p r m -> p (r m)")[:, 2 * NM + 512 * q:2 * NM + 512 * (q + 1)],
                               ps[:, (7, 4, 3)[q], :], ACT.Copy).then_inc(sem("cv_taken"), 1)
            for k in range(KT):
                act.wait_ge(sem("hp2_ready"), k + 1)
                act.activation(act_hi[:, k, 0:SEQ], hp2[:, k % 2, :], ACT.Identity, bias=mod[:, 48 + k, 8:9]).then_inc(sem("x3_hi"), 1)
                if k == 0:
                    act.wait_ge(sem("hs2_ready"), 1)
                    act.activation(act_hi[:, :, SEQ:T], mt2[:, 0, :].rearrange("p (k n) -> p k n", n=SAMP), ACT.Copy) \
                       .then_inc(sem("x3_hi_s"), 1)

            def take_up(u, which, nt, done):
                wait(act, sem("cv_saved"), 4 * nt)
                wait(act, sem("g_ready"), nt)
                b0 = 2 * which
                act.activation(up[which][:, 2:2 + HALF], ps[:, b0, 0:HALF], ACT.Copy).then_inc(done, 1)
                act.activation(up[which][:, 2 + HALF:2 + SEQ], ps[:, b0 + 1, 0:SEQ - HALF], ACT.Copy).then_inc(done, 1)
                act.activation(up_s[which][:, :, 2:10], ps[:, b0 + 1, SEQ - HALF:HALF].rearrange("p (b t) -> p b t", t=NS),
                               ACT.Copy).then_inc(done, 1)

            def up_tile(g, j):
                u, nt = ffn_up(g, j), G * g + j
                hi(u, 4)
                hi(u, 5)
                used(u, 2)
                take_up(u, 0, nt, sem("gate_out"))
                hi(u, 6)
                hi(u, 7)
                used(u, 4)
                take_up(u, 1, nt, sem("value_out"))
                act.wait_ge(sem("gate_conv"), nt + 1)
                act.activation(uc[0][:], uc[0][:], ACT.Gelu_apprx_tanh).then_inc(sem("gelu_done"), 1)
                act.wait_ge(sem("gp_ready"), nt + 1)
                act.activation(g_hi[:, bass.ds(j, 1), :].rearrange("p a n -> p (a n)"), gp[:], ACT.Copy).then_inc(sem("g_hi_ready"), 1)

            def down(g, last):
                def four(m, end=False):
                    u = ffn_down(g, m)
                    if not end:
                        for c in range(4):
                            hi(u, c + 4)
                with act.Fori(0, 3) as m:
                    four(m)
                four(3, last)

            def group(g, last=False):
                if isinstance(g, int) and g == 0:
                    up_tile(0, 0)
                    with act.Fori(1, G) as j:
                        up_tile(0, j)
                else:
                    with act.Fori(0, G) as j:
                        up_tile(g, j)
                down(g, last)
            group(0)
            with act.Fori(1, NG - 1) as g:
                group(g)
            group(NG - 1, True)

            for n in range(0, 24, 2):
                act.wait_ge(sem("y_turned"), n + 1)
                t, q = n // 4, n % 4
                w = P if t != 4 else SAMP
                if t < 5:
                    if t >= 2 and q == 0:
                        act.wait_ge(sem(f"y_stored{t % 2}"), 16 * (t // 2))
                    dst = yr[0:w, t % 2, q * 512:(q + 1) * 512]
                    act.activation(dst, ps[0:w, n % 8, :], ACT.Copy).then_inc(sem("y_even"), 1)
                else:
                    act.activation(crt[:, 4 * q:4 * q + 4, :], ps[:, n % 8, :].rearrange("p (a b) -> p a b", b=P), ACT.Copy).then_inc(sem("y_even"), 1)

        @block.vector
        def _(dve):
            ch = Chain(dve, sem("dve_steps"))

            def lo(u, k):
                s = k % SLOTS
                dve.wait_ge(hi_done, u[0] + (k + 1))
                dve.tensor_tensor(w_lo[s][:], raw[s][:], w_hi[s][:].bitcast(F32), ALU.subtract).then_inc(lo_done, 1)

            def take_rows(u, blocks, n):
                dve.wait_ge(blk_used, u[0] + blocks)
                dve.tensor_copy(mod_rows[:, 0:n, :], ps[0:2 * CB, 4, 0:P * n].rearrange("p (a b) -> p a b", b=P)) \
                   .then_inc(sem("rows_taken"), 1)

            def take_mod(n, m0, t, done=True):
                dve.wait_ge(sem("mod_turned"), t + 1)
                ins = dve.tensor_tensor(mod[:, bass.ds(m0, n), :], ps[:, 4, 448:448 + CB * n].rearrange("p (n c) -> p n c", c=CB),
                                        vec[:, bass.ds(m0, n)].unsqueeze(2).to_broadcast([P, n, CB]), ALU.add)
                if done:
                    ins.then_inc(sem("bank4_taken"), 1)

            dve.wait_ge(sem("c_turned"), 1)
            dve.wait_ge(sem("c_hi"), 1)
            dve.tensor_tensor(cs[:, :, CB:2 * CB], ps[:, 0, 0:KT * CB].rearrange("p (k c) -> p k c", c=CB),
                              cs[:, :, 0:CB].bitcast(F32), ALU.subtract).then_inc(sem("c_taken"), 1)
            dve.wait_ge(sem("vecs_turned"), 1)
            dve.tensor_copy(lst[:], ps[:, 3, 0:256]).then_inc(sem("vecs_taken"), 1)
            u = turn(B_ADA, 0, 8)
            for k in range(SLOTS):
                lo(u, k)
            for k in range(KT):
                dve.wait_ge(sem("x_turned"), k + 1)
                dve.tensor_copy(X[:, k, SEQ:T], ps[:, (7, 3)[k % 2], 0:SAMP]).then_inc(sem("x_taken_s"), 1)
            dve.wait_ge(sem("vecs_taken"), 3)
            dve.wait_ge(sem("bias_loaded"), 16)
            dve.wait_ge(sem("consts"), 1)

            def ada(i):
                u = turn(B_ADA, i, 8)
                for k in range(8):
                    lo(u, k + SLOTS)
                take_rows(u, 8, 4)
                take_mod(4, 4 * i, i)
            turns(dve, 8, ada)

            def modulate(s_, t_, v_, rstd, m_scale, m_shift, v_g, hs_sem):
                k4 = [P, KT, NB, NS]
                ch.link(dve.scalar_tensor_tensor(s_, mod[:, m_scale:m_scale + KT, :], 1.0,
                                                 vec[:, v_g:v_g + KT].unsqueeze(2).to_broadcast([P, KT, CB]), ALU.add, ALU.mult))
                ch.link(dve.tensor_tensor(v_.rearrange("p (k n) -> p k n", n=SAMP), X[:, :, SEQ:T],
                                          rstd[:, SEQ:T].unsqueeze(1).to_broadcast([P, KT, SAMP]), ALU.mult))
                t4 = t_.rearrange("p (k b t) -> p k b t", b=NB, t=NS)
                ch.link(dve.tensor_tensor(t4, v_.rearrange("p (k b t) -> p k b t", b=NB, t=NS),
                                          s_[:, :, 0:NB].unsqueeze(3).to_broadcast(k4), ALU.mult))
                dve.tensor_tensor(t4, t4, mod[:, m_shift:m_shift + KT, 0:NB].unsqueeze(3).to_broadcast(k4), ALU.add) \
                   .then_inc(hs_sem, 1)

            def modulated(s_, t_, halves, rstd, m_shift, names4):
                hp_ready, hi_sem, hi_s, ready = (sem(n) for n in names4)

                def scaled(k):
                    if k >= 2:
                        dve.wait_ge(ready, k - 1)
                    dve.scalar_tensor_tensor(halves[k % 2], X[:, k, 0:SEQ], s_[:, k, 8:9], rstd[:, 0:SEQ],
                                             ALU.mult, ALU.mult).then_inc(hp_ready, 1)
                scaled(0)
                for k in range(KT):
                    if k + 1 < KT:
                        scaled(k + 1)
                    if k == 0:
                        dve.wait_ge(hi_s, 1)
                        dve.tensor_tensor(act_lo[:, :, SEQ:T], t_.rearrange("p (k n) -> p k n", n=SAMP),
                                          act_hi[:, :, SEQ:T].bitcast(F32), ALU.subtract)
                    dve.wait_ge(hi_sem, k + 1)
                    dve.scalar_tensor_tensor(act_lo[:, k, 0:SEQ], halves[k % 2], mod[:, m_shift + k, 8:9],
                                             act_hi[:, k, 0:SEQ].bitcast(F32), ALU.add, ALU.subtract).then_inc(ready, 1)

            dve.wait_ge(sem("rs_ready"), 1)
            dve.wait_ge(sem("bank4_taken"), 8)
            ch.enter(0, 3)
            modulate(s1, mod_t, mod_u, rs, 16, 0, V_G1, sem("hs_ready"))
            ch.leave()
            ch.advance(3)
            modulated(s1, mod_t, hp, rs, 0, ("hp_ready", "x1_hi", "x1_hi_s", "x1_ready"))

            def softplus(i):
                dve.wait_ge(sem("scores_mm"), i)
                hb = bias_h[:, bass.ds(i - 1, 1)]
                for b, j0, n in ((5, 0, 512), (6, 512, 384), (7, 896, 384)):
                    ins = dve.tensor_scalar(zf[:, j0:j0 + n], ps[:, b, 0:n], SCALE, hb, ALU.mult, ALU.add)
                ins.then_inc(sem("z_taken"), 1)
                dve.wait_ge(sem("z_taken"), i)
                dve.wait_ge(sem("lz_ready"), i)
                dve.scalar_tensor_tensor(sp_[:], zf[:], 0.0, wt[:], ALU.max, ALU.add).then_inc(sem("sp_whole"), 1)
                dve.wait_ge(sem("sp_whole"), 2 * i - 1)
                dve.tensor_tensor(zf[:], zf[:], sp_[:], ALU.subtract).then_inc(sem("sp_whole"), 1)
                dve.wait_ge(sem("sp_whole"), 2 * i)
                for j in J0:
                    ins = dve.tensor_tensor(sp_[:, j:j + P], sp_[:, j:j + P], before[:], ALU.mult)
                ins.then_inc(sem("sp_ready"), 1)

            def log_weights(i):
                dve.wait_ge(sem("sums_mm"), i)
                dve.wait_ge(sem("sp_ready"), i)
                for b, j0, n in ((5, 0, 512), (6, 512, 384), (7, 896, 384)):
                    ins = dve.tensor_tensor(zf[:, j0:j0 + n], ps[:, b, 0:n], zf[:, j0:j0 + n], ALU.add)
                ins.then_inc(sem("arg_ready"), 1)
                dve.wait_ge(sem("w_exp"), i)
                for j in J0:
                    ins = dve.tensor_tensor(wt[:, j:j + P], wt[:, j:j + P], before[:], ALU.mult)
                ins.then_inc(sem("w_ready"), 1)

            def take_k(i):
                dve.wait_ge(sem("kv_turned"), i)
                if not isinstance(i, int) or i > 1:
                    dve.wait_ge(sem("k_stored"), 16 * i - 16)
                dve.tensor_copy(kn[:], ps[:, 3, :].rearrange("p (t d) -> p t d", d=P)).then_inc(sem("kn_taken"), 1)

            def take_sample(i):
                if not isinstance(i, int) or i > 1:
                    dve.wait_ge(sem("ks_stored"), 16 * i - 16)
                b4 = ps[0:SAMP, 4, :]
                h = bass.ds(i - 1, 1)
                dve.tensor_copy(vs[:, h, :].rearrange("p a d -> p (a d)"), b4[:, 128:256])
                dve.tensor_copy(ksn[:], b4[:, 256:384])
                dve.tensor_copy(zs[0:SAMP, h, :].rearrange("p a d -> p (a d)"), b4[:, 384:448]).then_inc(sem("bank4_taken"), 1)

            def qkv(i):
                u, prev = turn(B_QKV, i, 8), not starts(i)
                lo(u, 4)
                lo(u, 5)
                lo(u, 6)
                lo(u, 7)
                if prev:
                    dve.wait_ge(sem("scores_mm"), i)
                take_rows(u, 4, 1)
                if prev:
                    softplus(i)
                lo(u, 8)
                lo(u, 9)
                if prev:
                    log_weights(i)
                lo(u, 10)
                if prev:
                    take_k(i)
                lo(u, 11)
                take_mod(1, i + 32, i + 8, done=not prev)
                if prev:
                    take_sample(i)
                dve.wait_ge(sem("rq_ready"), i + 1)
                dve.scalar_tensor_tensor(qf[:], qraw[:], vec[:, V_GQ:V_GQ + 1], sqq[:], ALU.mult, ALU.mult) \
                   .then_inc(sem("qf_ready"), 1)
                dve.wait_ge(sem("qf_ready"), i + 1)
                dve.tensor_copy(qs[:, bass.ds(i, 1), :].rearrange("p a n -> p (a n)"), qf[:, SEQ:T])
                dve.wait_ge(sem("rk_ready"), i + 1)
                dve.scalar_tensor_tensor(kf[:], kraw[:], vec[:, V_GK:V_GK + 1], sqk[:], ALU.mult, ALU.mult) \
                   .then_inc(sem("qk_ready"), 1)
            turns(dve, NH, qkv, 2)
            softplus(NH)
            log_weights(NH)
            take_k(NH)
            take_sample(NH)

            dve.wait_ge(sem("x_saved"), 16)
            dve.wait_ge(sem("zs_zeroed"), 1)
            dve.wait_ge(sem("o_taken"), NH)
            dve.wait_ge(sem("v_stored"), 16 * NH)
            dve.wait_ge(sem("k_stored"), 16 * NH)
            dve.wait_ge(sem("ks_stored"), 16 * NH)
            dve.wait_ge(sem("bank4_taken"), 17)
            z3, zf_ = zs[0:SAMP], zs[0:SAMP].rearrange("p h q -> p (h q)")
            same3 = same[:].unsqueeze(1).to_broadcast([SAMP, NH, SAMP])
            ch.enter(0, 5)
            dve.scalar_tensor_tensor(z3, z3, SCALE, bias_h[0:SAMP, :].unsqueeze(2).to_broadcast([SAMP, NH, SAMP]),
                                     ALU.mult, ALU.add).then_inc(sem("self_z"), 1)
            dve.wait_ge(sem("self_z"), 1)
            dve.wait_ge(sem("self_l"), 1)
            ch.link(dve.scalar_tensor_tensor(wself[:], zf_, 0.0, wself[:], ALU.max, ALU.add))
            ch.link(dve.tensor_tensor(spc[0:SAMP, :], zf_, wself[:], ALU.subtract))
            w3 = wself[:].rearrange("p (h q) -> p h q", q=SAMP)
            dve.tensor_tensor(z3, w3, same3, ALU.mult).then_inc(sem("self_sp_ready"), 1)
            dve.wait_ge(sem("self_mm"), 1)
            dve.wait_ge(sem("self_sp_ready"), 1)
            dve.tensor_tensor(spc[0:SAMP, :], ps[0:SAMP, 7, :], spc[0:SAMP, :], ALU.add).then_inc(sem("self_arg"), 1)
            dve.wait_ge(sem("self_w"), 1)
            dve.tensor_tensor(w3, w3, same3, ALU.mult).then_inc(sem("self_done"), 1)
            dve.wait_ge(sem("c8_parts"), 1)
            ch.link(dve.tensor_tensor(c8[:, 0, :], c8[:, 0, :], c8[:, 1, :], ALU.add))
            ch.link(dve.tensor_scalar(c8[:, 1, :], c8[:, 0, :], LRU_C, None, ALU.mult))
            ch.link(dve.tensor_scalar(c8[:, 0, :], c8[:, 0, :], -LRU_C, None, ALU.mult))
            dve.memset(xlp[:, 0:3], 0.0).then_inc(sem("c8_ready"), 1)
            dve.wait_ge(sem("c8_ready"), 1)
            ch.leave()
            ch.advance(5)

            xd = xlp[:, 3:3 + T]

            def recurrence_a(i):
                dve.wait_ge(sem("a_ready"), 2 * i)
                ch.link(dve.tensor_tensor(La[:], Lc[:], Lc[:], ALU.mult))
                dve.scalar_tensor_tensor(xd, La[:], 1.0, xd, ALU.add, ALU.mult).then_inc(sem("m2_ready"), 1)
                dve.wait_ge(sem("i_taken"), i)
                ch.link(dve.tensor_tensor(Lb[:], Lb[:], xc[:], ALU.mult))

            def recurrence_b(i):
                n = i - 1
                dve.wait_ge(sem("m_ready"), i)
                ch.link(dve.memset(xd[:, 0:1], 1.0))
                ch.link(dve.tensor_tensor(Lb[:], Lb[:], xd, ALU.mult))
                a_s = Lc[:, SEQ:T].rearrange("p (b t) -> p b t", t=NS)[:, :, 0:1]
                b_s = Lb[:, SEQ:T].rearrange("p (b t) -> p b t", t=NS)[:, :, 0:1]
                h0 = lst[:, 192:256].rearrange("p (b n) -> p b n", n=NL)[:, :, bass.ds(n, 1)]
                t8 = La[:, 0:NB].unsqueeze(2)
                ch.link(dve.tensor_tensor(t8, a_s, h0, ALU.mult))
                ch.link(dve.tensor_tensor(b_s, b_s, t8, ALU.add))
                ch.link(dve.memset(a_s, 0.0))
                ch.step(dve.tensor_tensor_scan(xc[:, 0:SEQ], Lc[:, 0:SEQ], Lb[:, 0:SEQ], 0.0, ALU.mult, ALU.add))
                ch.link(dve.tensor_tensor_scan(xc[:, SEQ:T], Lc[:, SEQ:T], Lb[:, SEQ:T], 0.0, ALU.mult, ALU.add))
                dve.tensor_copy(lnew[:, bass.ds(n + 216, 1)], xc[:, SEQ - 1:SEQ])
                dve.tensor_copy(lnew[:, 224:288].rearrange("p (b n) -> p b n", n=NL)[:, :, bass.ds(n, 1)],
                                xc[:, SEQ:T].rearrange("p (b t) -> p b t", t=NS)[:, :, NS - 1:NS])
                dve.wait_ge(sem("gl_out"), i)
                dve.tensor_tensor(X[:, bass.ds(n + NH, 1), :].rearrange("p a n -> p (a n)"), xc[:], gg[:], ALU.mult) \
                   .then_inc(sem("lru_done"), 1)

            def take_keys(i, s):
                dve.wait_ge(sem("kb_turned"), 8 * i + (s + 1))
                wait(dve, sem("kb_used"), 8 * i + s)
                dve.tensor_copy(kt_[1][:], ps[:, 5, :].rearrange("p (h k) -> p h k", k=P)).then_inc(sem("kb_taken"), 1)

            def take_scores(i):
                dve.wait_ge(sem("ka_used"), 8 * i)
                dve.wait_ge(sem("kb_used"), 8 * i)
                for s in range(PAGES):
                    c = slice(s * 64, (s + 1) * 64)
                    ins = dve.scalar_tensor_tensor(zc[:, c].rearrange("p (h q) -> p h q", q=NS),
                                                   ps[:, 7, c].rearrange("p (h q) -> p h q", q=NS), SCALE,
                                                   bias_h[:].unsqueeze(2).to_broadcast([P, NH, NS]), ALU.mult, ALU.add)
                ins.then_inc(sem("zc_taken"), 1)

            def softplus_pages(i):
                dve.wait_ge(sem("zc_taken"), i)
                dve.wait_ge(sem("lc_ready"), i)
                ch.link(dve.scalar_tensor_tensor(spc[:], zc[:], 0.0, spc[:], ALU.max, ALU.add))
                ch.step(dve.tensor_tensor(zc[:], zc[:], spc[:], ALU.subtract))
                wait(dve, sem("o2_mm"), i - 1)
                ch.link(dve.tensor_copy(suf[:, 448:512].rearrange("p (h q) -> p h q", q=NS), zs[:, :, bass.ds(NS * i - NS, NS)]))
                for s in range(6, -1, -1):
                    ins = dve.tensor_tensor(suf[:, s * 64:(s + 1) * 64], suf[:, (s + 1) * 64:(s + 2) * 64],
                                            spc[:, (s + 1) * 64:(s + 2) * 64], ALU.add)
                    if s:
                        ch.link(ins)
                    else:
                        ins.then_inc(sem("spc_ready"), 1)

            def page_args(i):
                dve.wait_ge(sem("sums2_mm"), i)
                dve.tensor_tensor(zc[:], ps[:, 6, :], zc[:], ALU.add).then_inc(sem("argc_ready"), 1)

            def pads(i):
                dve.wait_ge(sem("xl_out"), 3 * i + 3)
                ch.link(dve.tensor_copy(xlp_s[:, :, 0:3], lst[:, 0:192].rearrange("p (b w n) -> p b w n", w=3, n=NL)
                                        [:, :, :, bass.ds(i, 1)].rearrange("p b w n -> p b (w n)")))

            def tap(i, w):
                xc_s = xc[:, SEQ:T].rearrange("p (b t) -> p b t", t=NS)
                col = vec[:, bass.ds(V_LCW + w * NL + i, 1)]
                if w == 3:
                    bcol = vec[:, bass.ds(V_LCB + i, 1)]
                    ch.step(dve.tensor_scalar(xc[:, 0:SEQ], xlp[:, w:w + SEQ], col, bcol, ALU.mult, ALU.add))
                    ch.link(dve.tensor_scalar(xc_s, xlp_s[:, :, w:w + NS], col, bcol, ALU.mult, ALU.add))
                else:
                    ch.step(dve.scalar_tensor_tensor(xc[:, 0:SEQ], xlp[:, w:w + SEQ], col, xc[:, 0:SEQ], ALU.mult, ALU.add))
                    ins = dve.scalar_tensor_tensor(xc_s, xlp_s[:, :, w:w + NS], col, xc_s, ALU.mult, ALU.add)
                    if w:
                        ch.link(ins)
                    else:
                        ins.then_inc(sem("xc_ready"), 1)

            PS, CS = 18, 8

            def lru(i):
                u, prev = turn(B_LRU, i, 16), not starts(i)
                ch.enter((PS + CS) * i - PS, PS + CS) if prev else ch.enter(0, CS)
                if prev:
                    take_scores(i)
                take_keys(i, 0)
                if prev:
                    softplus_pages(i)
                    take_mod(3, 6 * i + 37, 2 * i + 15)
                take_keys(i, 1)
                for k in range(4, 8):
                    lo(u, k)
                if prev:
                    recurrence_a(i)
                    page_args(i)
                take_keys(i, 2)
                take_keys(i, 3)
                lo(u, 8)
                if prev:
                    recurrence_b(i)
                for k in range(9, 12):
                    lo(u, k)
                take_rows(u, 8, 3)
                take_keys(i, 4)
                pads(i)
                tap(i, 3)
                take_mod(3, 6 * i + 40, 2 * i + 16)
                tap(i, 2)
                take_keys(i, 5)
                tap(i, 1)
                tap(i, 0)
                for k in range(12, 16):
                    lo(u, k)
                take_keys(i, 6)
                take_keys(i, 7)
                for k in range(16, 20):
                    lo(u, k)
                take_rows(u, 16, 3)
                ch.leave()
            turns(dve, NL, lru, 2)
            ch.advance((PS + CS) * NL - PS)
            ch.enter(0, PS)
            take_scores(NL)
            softplus_pages(NL)
            recurrence_a(NL)
            page_args(NL)
            recurrence_b(NL)
            take_mod(3, 6 * NL + 37, 2 * NL + 15)
            ch.leave()
            ch.advance(PS)

            dve.wait_ge(sem("lru_done"), NL)
            for k in range(KT):
                dve.wait_ge(sem("mix_hi"), k + 1)
                dve.tensor_tensor(act_lo[:, k, :], X[:, k, :], act_hi[:, k, :].bitcast(F32), ALU.subtract) \
                   .then_inc(sem("mix_ready"), 1)

            def gated(m, bank, gate, gate_s, base, base_s, t, done):
                tile_ = X[:, bass.ds(m, 1), :].rearrange("p a n -> p (a n)")
                dve.tensor_tensor(t, ps[:, bank + 1, SEQ - HALF:HALF].rearrange("p (b t) -> p b t", t=NS),
                                  gate_s.to_broadcast([P, NB, NS]), ALU.mult).then_inc(sem("gated_part"), 1)
                dve.scalar_tensor_tensor(tile_[:, 0:HALF], ps[:, bank, 0:HALF], gate, base[:, 0:HALF], ALU.mult, ALU.add)
                dve.scalar_tensor_tensor(tile_[:, HALF:SEQ], ps[:, bank + 1, 0:SEQ - HALF], gate, base[:, HALF:SEQ],
                                         ALU.mult, ALU.add)
                return dve.tensor_tensor, (tile_[:, SEQ:T].rearrange("p (b t) -> p b t", t=NS), t, base_s, ALU.add)

            def out(i):
                u = turn(B_OUT, i, 12)
                for j in range(4):
                    k, m = (0, 2, 6, 8)[j], 4 * i + j
                    lo(u, k + 4)
                    lo(u, k + 5)
                    if j % 2:
                        lo(u, k + 6)
                        lo(u, k + 7)
                    dve.wait_ge(blk_used, u[0] + (k + 2))
                    dve.wait_ge(sem(f"xres_loaded{j % 2}"), 32 * i + 16 * (j // 2 + 1))
                    if isinstance(i, int) and j == 0:
                        dve.wait_ge(sem("mix_ready"), KT)
                    base = xres[:, j % 2, :]
                    gt = mod[:, bass.ds(4 * i + (32 + j), 1), :].rearrange("p a c -> p (a c)")
                    f, a = gated(m, 2 * (j % 2), gt[:, 8:9], gt[:, 0:NB].unsqueeze(2), base,
                                 base[:, SEQ:T].rearrange("p (b t) -> p b t", t=NS),
                                 t64[:, j % 2, :].rearrange("p (b t) -> p b t", t=NS), None)
                    dve.wait_ge(sem("gated_part"), 4 * i + (j + 1))
                    f(*a).then_inc(sem("x2_ready"), 1)
                take_rows(u, 12, 2)
                take_mod(2, 88 + 2 * i, 32 + i)
            turns(dve, 4, out)

            dve.wait_ge(sem("rs2_ready"), 1)
            dve.wait_ge(sem("x2_ready"), KT)
            dve.wait_ge(sem("bank4_taken"), 37)
            dve.wait_ge(blk_used, B_FFN)
            ch.enter(0, 3)
            modulate(s2[:], mt2[:, 0, :], mt2[:, 1, :], rs2, 64, 48, V_G2, sem("hs2_ready"))
            ch.leave()
            ch.advance(3)
            modulated(s2, mt2[:, 0, :], [hp2[:, 0, :], hp2[:, 1, :]], rs2, 48, ("hp2_ready", "x3_hi", "x3_hi_s", "x3_ready"))
            dve.wait_ge(sem("lnew_turned"), 1)
            dve.tensor_copy(crl[:, 0:256], ps[:, 2, 0:256]).then_inc(sem("lnew_taken"), 1)
            dve.tensor_copy(crl[0:32, 256:384], ps[0:32, 2, 256:384]).then_inc(sem("lnew_taken"), 1)

            dve.wait_ge(sem("x3_ready"), KT)
            for w in range(2):
                dve.memset(up[w][:, 0:2], 0.0)
            dve.wait_ge(sem("cv_taken"), 3)

            def convolve(which, nt, out_sem, done):
                dve.wait_ge(out_sem, 3 * nt + 3)
                m = nt + NFF * which
                ch.link(dve.tensor_copy(up_s[which][:, :, 0:2], cv[:, 2:18, bass.ds(m, 1)].rearrange("p (b w) c -> p b (w c)", w=2)))
                uc_s = uc[which][:, SEQ:T].rearrange("p (b t) -> p b t", t=NS)
                for w in (2, 1, 0):
                    col = vec[:, bass.ds(m + (V_FCW + w * NM), 1)]
                    if w == 2:
                        bcol = vec[:, bass.ds(m + V_FCB, 1)]
                        ch.step(dve.tensor_scalar(uc[which][:, 0:SEQ], up[which][:, w:w + SEQ], col, bcol, ALU.mult, ALU.add))
                        ch.link(dve.tensor_scalar(uc_s, up_s[which][:, :, w:w + NS], col, bcol, ALU.mult, ALU.add))
                    else:
                        ch.step(dve.scalar_tensor_tensor(uc[which][:, 0:SEQ], up[which][:, w:w + SEQ], col,
                                                         uc[which][:, 0:SEQ], ALU.mult, ALU.add))
                        ins = dve.scalar_tensor_tensor(uc_s, up_s[which][:, :, w:w + NS], col, uc_s, ALU.mult, ALU.add)
                        if w:
                            ch.link(ins)
                        else:
                            ins.then_inc(done, 1)

            def up_tile(g, j):
                u, nt = ffn_up(g, j), G * g + j
                ch.enter(12 * nt, 12)
                lo(u, 4)
                lo(u, 5)
                convolve(0, nt, sem("gate_out"), sem("gate_conv"))
                lo(u, 6)
                lo(u, 7)
                convolve(1, nt, sem("value_out"), sem("value_conv"))
                dve.wait_ge(sem("value_conv"), nt + 1)
                dve.wait_ge(sem("gelu_done"), nt + 1)
                dve.tensor_tensor(gp[:], uc[0][:], uc[1][:], ALU.mult).then_inc(sem("gp_ready"), 1)
                dve.wait_ge(sem("gp_ready"), nt + 1)
                dve.wait_ge(sem("g_hi_ready"), nt + 1)
                h = bass.ds(j, 1)
                dve.tensor_tensor(g_lo[:, h, :].rearrange("p a n -> p (a n)"), gp[:],
                                  g_hi[:, h, :].rearrange("p a n -> p (a n)").bitcast(F32), ALU.subtract).then_inc(sem("g_ready"), 1)
                ch.leave()

            def down(g, last):
                def four(m, end=False):
                    u = ffn_down(g, m)
                    for c in range(4):
                        if not end:
                            lo(u, c + 4)
                        mm = 4 * m + c
                        tiles = KT * g + mm
                        dve.wait_ge(blk_used, u[0] + (c + 1))
                        wait(dve, sem("y_taken"), tiles)
                        tile_ = X[:, bass.ds(mm, 1), :].rearrange("p a n -> p (a n)")
                        gt = mod[:, bass.ds(mm + 80, 1), :].rearrange("p a c -> p (a c)")
                        ts_ = tile_[:, SEQ:T].rearrange("p (b t) -> p b t", t=NS)
                        f, a = gated(mm, 2 * (c % 2), gt[:, 8:9], gt[:, 0:NB].unsqueeze(2), tile_, ts_,
                                     t64b[:, c % 2, :].rearrange("p (b t) -> p b t", t=NS), None)
                        dve.wait_ge(sem("gated_part"), tiles + (KT + 1))
                        f(*a).then_inc(sem("y_taken"), 1)
                four(0)
                with dve.Fori(1, 3) as m:
                    four(m)
                four(3, last)

            def group(g, last=False):
                if isinstance(g, int) and g == 0:
                    up_tile(0, 0)
                    with dve.Fori(1, G) as j:
                        up_tile(0, j)
                else:
                    with dve.Fori(0, G) as j:
                        up_tile(g, j)
                down(g, last)
            group(0)
            with dve.Fori(1, NG - 1) as g:
                group(g)
            group(NG - 1, True)

            for n in range(1, 24, 2):
                dve.wait_ge(sem("y_turned"), n + 1)
                t, q = n // 4, n % 4
                w = P if t != 4 else SAMP
                if t < 5:
                    if t >= 2 and q == 1:
                        dve.wait_ge(sem(f"y_stored{t % 2}"), 16 * (t // 2))
                    dve.tensor_copy(yr[0:w, t % 2, q * 512:(q + 1) * 512], ps[0:w, n % 8, :]).then_inc(sem("y_odd"), 1)
                elif q == 1:
                    dve.tensor_copy(crt[:, 4:8, :], ps[:, n % 8, :].rearrange("p (a b) -> p a b", b=P)).then_inc(sem("y_odd"), 1)
                else:
                    dve.tensor_copy(crt[:, 12, :], ps[:, n % 8, 0:P])
                    dve.tensor_copy(crt[0:64, 13, :], ps[0:64, n % 8, P:2 * P]).then_inc(sem("y_odd"), 1)

        @block.gpsimd
        def _(pool):
            def hold(name, value):
                wait(pool, sem(name), value)
                if not isinstance(value, int):
                    pool.sem_inc(sem("pool_waits"), 1)

            pool.memset(X[0:CB].rearrange("p k n -> p (k n)")[:, 0:D], 0.0).then_inc(sem("zeroed"), 1)
            pool.memset(vr[:, 1, :], 0.0).then_inc(sem("zeroed"), 1)
            pool.memset(eps[:], EPS)
            pool.memset(neg_ones[:], -1.0)
            pool.memset(ident[:], 0.0)
            pool.memset(neg_later[:], -1.0)
            pool.memset(before[:], 1.0)
            pool.memset(same[:], 1.0).then_inc(sem("filled"), 1)
            pool.wait_ge(sem("filled"), 1)
            pool.affine_select(out=ident[:], in_=ident[:], compare_op=ALU.not_equal, fill=1.0, base=0,
                               pattern=[[-1, P]], channel_multiplier=1)
            pool.memset(sel[:], 0.0).then_inc(sem("sel_zeroed"), 1)
            pool.wait_ge(sem("sel_zeroed"), 1)
            for d in (0, CB):
                ins = pool.affine_select(out=sel[:], in_=sel[:], compare_op=ALU.not_equal, fill=1.0, base=-d,
                                         pattern=[[-1, CB]], channel_multiplier=1)
                ins.then_inc(sem("sel_zeroed"), 1)
                pool.wait_ge(sem("sel_zeroed"), 2 + d // CB)
            pool.affine_select(out=neg_later[:], in_=neg_later[:], compare_op=ALU.is_gt, fill=0.0, base=0,
                               pattern=[[-1, P]], channel_multiplier=1)
            pool.affine_select(out=before[:], in_=before[:], compare_op=ALU.is_gt, fill=0.0, base=0,
                               pattern=[[1, P]], channel_multiplier=-1)
            same3 = same[:].rearrange("p (b t) -> p b t", t=NS)
            pool.affine_select(out=same3, in_=same3, compare_op=ALU.is_gt, fill=0.0, base=0,
                               pattern=[[NS, NB], [1, NS]], channel_multiplier=-1).then_inc(sem("filled"), 1)
            pool.wait_ge(sem("filled"), 2)
            pool.affine_select(out=same3, in_=same3, compare_op=ALU.is_ge, fill=0.0, base=0,
                               pattern=[[-NS, NB], [0, NS]], channel_multiplier=1).then_inc(sem("consts"), 1)
            pool.dma_start(bias_h[:], b_sb.to_broadcast([P, NH])).then_inc(sem("bias_loaded"), 16)
            pool.wait_ge(sem("bias_loaded"), 16)
            pool.wait_ge(sem("x1_ready"), KT)
            pool.memset(zs[SAMP:P], 0.0).then_inc(sem("zs_zeroed"), 1)

            kpo = k_prompt[0, 0].rearrange("t p h d -> p t h d")
            vpo = v_prompt[0, 0].rearrange("t p h d -> p t h d")
            kso = k_sample[0].rearrange("b t h d -> (b t) h d")
            vso = v_sample[0].rearrange("b t h d -> (b t) h d")

            def store(i):
                h = bass.ds(i - 1, 1)
                hold("vn_taken", i)
                pool.dma_start(vpo[:, :, h, :].rearrange("p t h d -> p t (h d)"), vn[:]).then_inc(sem("v_stored"), 16)
                hold("kn_taken", i)
                pool.dma_start(kpo[:, :, h, :].rearrange("p t h d -> p t (h d)"), kn[:]).then_inc(sem("k_stored"), 16)
                hold("bank4_taken", i + 9)
                pool.dma_start(kso[:, h, :].rearrange("p h d -> p (h d)"), ksn[:]).then_inc(sem("ks_stored"), 16)
            with pool.Fori(1, NH + 1) as i:
                store(i)
            pool.dma_start(vso.rearrange("p h d -> p (h d)"), vs[:].rearrange("p h d -> p (h d)")).then_inc(sem("vs_stored"), 16)

            pool.wait_ge(sem("self_z"), 1)
            pool.dma_start(pt[:], page_table.rearrange("b p -> (b p)").unsqueeze(0)).then_inc(sem("pt_loaded"), 16)
            pool.wait_ge(sem("pt_loaded"), 16)
            ck = cache_k[0].rearrange("n p h d -> n p (h d)")
            cvv = cache_v[0].rearrange("n p h d -> n p (h d)")
            npool = cache_k.shape[1]

            def page(i, s):
                return pool.value_load(pt[0:1, bass.ds(8 * i + s, 1)], min_val=0, max_val=npool - 1)

            def fetch(dst, src, v, name):
                pool.dma_start(dst[:].rearrange("p h d -> p (h d)"),
                               src[bass.ds(v, 1)].rearrange("n p c -> p (n c)")).then_inc(sem(name), 16)

            def load_k(i, s):
                v = page(i, s)
                hold("kb_turned", 8 * i + (s - 1))
                fetch(kpg[s % 2], ck, v, f"k_loaded{s % 2}")

            def load_v(i, s):
                v = page(i - 1, s)
                hold("v_used", 8 * i + (s - 9))
                fetch(vpg[s % 2], cvv, v, f"v_loaded{s % 2}")

            def gates(i):
                hold("i_mm", i)
                pool.dma_start(wg[:, 0, :], w_lru_a[0, bass.ds(i, 1)].rearrange("a c d -> c (a d)")).then_inc(sem("gates_loaded"), 16)
                pool.dma_start(wg[:, 1, :], w_lru_x[0, bass.ds(i, 1)].rearrange("a c d -> c (a d)")).then_inc(sem("gates_loaded"), 16)

            def save(i):
                pool.wait_ge(sem("xl_out"), 3 * i + 3)
                pool.tensor_copy(lnew[:, 0:24].rearrange("p (r n) -> p r n", n=NL)[:, :, bass.ds(i, 1)],
                                 xlp[:, SEQ:SEQ + 3].unsqueeze(2)).then_inc(sem("lnew_saved"), 1)
                pool.tensor_copy(lnew[:, 24:216].rearrange("p (b w n) -> p b w n", w=3, n=NL)[:, :, :, bass.ds(i, 1)]
                                 .rearrange("p b w n -> p b (w n)"), xlp_s[:, :, 8:11]).then_inc(sem("lnew_saved"), 1)

            def lru(i):
                prev = not starts(i)
                more = not (isinstance(i, int) and i == NL - 1)
                load_k(i, 2)
                load_k(i, 3)
                if prev:
                    load_v(i, 2)
                load_k(i, 4)
                if prev:
                    load_v(i, 3)
                load_k(i, 5)
                if prev:
                    load_v(i, 4)
                save(i)
                if prev:
                    load_v(i, 5)
                load_k(i, 6)
                if prev:
                    load_v(i, 6)
                load_k(i, 7)
                if prev:
                    load_v(i, 7)
                if more:
                    load_k(i + 1, 0)
                load_v(i + 1, 0)
                if more:
                    load_k(i + 1, 1)
                load_v(i + 1, 1)
                if more:
                    gates(i + 1)
            gates(0)
            load_k(0, 0)
            load_k(0, 1)
            lru(0)
            with pool.Fori(1, NL - 1) as i:
                lru(i)
            lru(NL - 1)
            for s in range(2, PAGES):
                load_v(NL, s)

            pool.wait_ge(sem("lru_done"), NL)
            pool.wait_ge(sem("o2_taken"), NL)
            pool.wait_ge(sem("vs_stored"), 16)
            pool.dma_start(str_[:], state_ffn_conv.rearrange("a b w (r c) -> (a b w r) c", c=P)
                           .rearrange("(j p) c -> p j c", p=P)).then_inc(sem("ffn_state_loaded"), 16)
            xs_v = x_save.rearrange("p (k n) -> p k n", n=T)
            pool.wait_ge(sem("x_saved"), 16)

            def residual(i):
                for j in range(4):
                    hold("x2_ready", 4 * i + (j - 1))
                    pool.dma_start(xres[:, j % 2, :], xs_v[:, bass.ds(4 * i + j, 1), :].rearrange("p a n -> p (a n)")) \
                        .then_inc(sem(f"xres_loaded{j % 2}"), 16)
            turns(pool, 4, residual)

            stored = sem("states_stored")
            pool.wait_ge(sem("lnew_taken"), 2)
            cl = lru_conv_prompt.rearrange("a b w (r c) -> (a b w r) c", c=P)
            cls = lru_conv_sample.rearrange("a b w (r c) -> (a b w r) c", c=P)
            hs = lru_h_sample.rearrange("a b (r c) -> (a b r) c", c=P)
            pool.dma_start(cl, crl[0:24, 0:P]).then_inc(stored, 16)
            pool.dma_start(cls[0:104], crl[24:128, 0:P]).then_inc(stored, 16)
            pool.dma_start(cls[104:192], crl[0:88, P:2 * P]).then_inc(stored, 16)
            pool.dma_start(lru_h_prompt.rearrange("a b (r c) -> (a b r) c", c=P), crl[88:96, P:2 * P]).then_inc(stored, 16)
            pool.dma_start(hs[0:32], crl[96:128, P:2 * P]).then_inc(stored, 16)
            pool.dma_start(hs[32:64], crl[0:32, 2 * P:3 * P]).then_inc(stored, 16)
            pool.wait_ge(stored, 96)

            def save(which, nt, conv_sem, out_sem):
                pool.wait_ge(conv_sem, nt + 1)
                m = bass.ds(nt + NFF * which, 1)
                pool.tensor_copy(cv[:, 0:2, m], up[which][:, SEQ:SEQ + 2].unsqueeze(2)).then_inc(sem("cv_saved"), 1)
                pool.tensor_copy(cv[:, 2:18, m].rearrange("p (b w) c -> p b (w c)", w=2), up_s[which][:, :, 8:10]).then_inc(sem("cv_saved"), 1)

            def states(nt):
                save(0, nt, sem("gate_conv"), None)
                save(1, nt, sem("value_conv"), None)
            turns(pool, NFF, states)

            pool.wait_ge(sem("y_even"), 12)
            pool.wait_ge(sem("y_odd"), 12)
            fp = ffn_conv_prompt.rearrange("a b w (r c) -> (a b w r) c", c=P)
            fs = ffn_conv_sample.rearrange("a b w (r c) -> (a b w r) c", c=P)
            pool.dma_start(fp[0:128], crt[:, 0, :]).then_inc(stored, 16)
            pool.dma_start(fp[128:192], crt[0:64, 1, :]).then_inc(stored, 16)
            pool.dma_start(fs[0:64], crt[64:128, 1, :]).then_inc(stored, 16)
            pool.dma_start(fs[64:64 + 11 * P].rearrange("(j p) c -> p j c", p=P), crt[:, 2:13, :]).then_inc(stored, 16)
            pool.dma_start(fs[64 + 11 * P:1536], crt[0:64, 13, :]).then_inc(stored, 16)
            pool.wait_ge(stored, 176)


_INS = ['x_prompt', 'x_sample', 'c_prompt', 'c_sample', 'cache_k', 'cache_v', 'page_table',
        'state_lru_conv', 'state_lru_h', 'state_ffn_conv',
        'w_ada', 'b_ada', 'g_norm1', 'w_in', 'g_q', 'g_k', 'b_sb', 'w_lru_conv', 'b_lru_conv',
        'w_lru_a', 'b_lru_a', 'w_lru_x', 'b_lru_x', 'lru_lambda', 'w_out',
        'g_norm2', 'w_up', 'w_ffn_conv', 'b_ffn_conv', 'w_down']
_OUTS = [(1, 512, 2048), (8, 8, 2048), (1, 1, 4, 128, 8, 128), (1, 1, 4, 128, 8, 128), (1, 8, 8, 8, 128),
         (1, 8, 8, 8, 128), (1, 1, 3, 1024), (1, 8, 3, 1024), (1, 1, 1024), (1, 8, 1024),
         (1, 1, 2, 12288), (1, 8, 2, 12288)]


def kernel(**inputs):
    import numpy as _np
    import concourse.bacc as _bacc
    from concourse import mybir as _mybir
    from concourse.bass_utils import run_bass_kernel_spmd as _run

    nc = _bacc.Bacc("TRN2", target_bir_lowering=False, num_devices=1, dynamic_dma_scratch_size=2560)
    arrays, args = {}, []
    for name in _INS:
        a = _np.ascontiguousarray(inputs[name])
        arrays[f"in_{name}_dram"] = a
        args.append(nc.dram_tensor(f"in_{name}_dram", a.shape, _mybir.dt.from_np(a.dtype), kind="ExternalInput").ap())
    for i, shape in enumerate(_OUTS):
        args.append(nc.dram_tensor(f"out_{i}_dram", shape, F32, kind="ExternalOutput").ap())
    build(nc, *args)
    r = _run(nc, [arrays], core_ids=[0])
    return tuple(r.results[0][f"out_{i}_dram"] for i in range(len(_OUTS)))
```
